# Optimizing a Trainium2 kernel written in Bass

```python
import math
import jax, jax.numpy as jnp
from jax import lax
import numpy as np

D_MODEL = 1024
BATCH = 1
SEQ = 256
DEPTH = 1
DEC_BATCH = 8
DEC_SEQ = 4
PAST_LEN = 2048
PAGE_SIZE = 128

MIX_WIDTH = D_MODEL
A_HEADS = 4
A_DK = 128
A_DV = 128
A_WIDTH = A_HEADS * A_DK
HGRN_CHUNK = 64
B_WIDTH = MIX_WIDTH - A_WIDTH
B_GROUPS = 4
B_CH = B_WIDTH // B_GROUPS
GMLP_CHUNK = 128
IN_COLS = 4 * A_WIDTH + 2 * B_WIDTH
MEM_LEN = 256
X_HEADS = 4
X_HD = D_MODEL // X_HEADS
N_EXPERTS = 32
TOP_K = 4
D_FF = D_MODEL
SWIGLU_LIMIT = 7.0
SWIGLU_ALPHA = 1.702
MOE_BLOCK = 128
EPS = 1e-6

kernel_name = "hymba_hgrn2_gmlp_xmem_moe_step"

def rms_norm(x, g):
    xf = x.astype(jnp.float32)
    y = xf * lax.rsqrt(jnp.mean(xf * xf, axis=-1, keepdims=True) + EPS)
    return (y * g.astype(jnp.float32)).astype(x.dtype)

def hgrn2_recurrence(q, k, v, logf, S0):
    f32 = jnp.float32
    Bn, L, H, _ = q.shape
    DV = v.shape[-1]
    c = math.gcd(L, HGRN_CHUNK)
    n = L // c

    def chunks(t):
        return t.astype(f32).reshape(Bn, n, c, H, t.shape[-1]).transpose(1, 0, 3, 2, 4)

    causal = jnp.tril(jnp.ones((c, c), dtype=bool))[:, :, None]

    def step(S, inp):
        qc, kc, vc, gc = inp
        b = jnp.cumsum(gc, axis=2)
        o_inter = jnp.einsum("bhtk,bhkv->bhtv", qc * jnp.exp(b), S)
        rel = b[:, :, :, None, :] - b[:, :, None, :, :]
        decay = jnp.exp(jnp.where(causal, rel, -jnp.inf))
        scores = jnp.einsum("bhtk,bhsk,bhtsk->bhts", qc, kc, decay)
        o_intra = jnp.einsum("bhts,bhsv->bhtv", scores, vc)
        b_end = b[:, :, -1:, :]
        S_new = (jnp.exp(b_end[:, :, 0, :])[..., None] * S
                 + jnp.einsum("bhsk,bhsv->bhkv", kc * jnp.exp(b_end - b), vc))
        return S_new, o_inter + o_intra

    S_fin, o = lax.scan(step, S0.astype(f32), (chunks(q), chunks(k), chunks(v), chunks(logf)))
    o = o.transpose(1, 0, 3, 2, 4).reshape(Bn, L, H, DV)
    return o, S_fin

def gmlp_spatial(u, vn, w_s, b_s):
    Bn, L, G, C = u.shape
    c = min(L, GMLP_CHUNK)
    n = L // c
    w = jnp.tril(w_s[:, :c, :c])
    vc = vn.reshape(Bn, n, c, G, C)
    s = jnp.einsum("gts,bnsgc->bntgc", w, vc) + b_s[:, :c].T[None, None, :, :, None]
    return u * s.reshape(Bn, L, G, C).astype(u.dtype)

def token_mixer(h, S0, lb, w_in, w_out, hgrn_norm_g, gmlp_ln_g, gmlp_ln_b, gmlp_w_s, gmlp_b_s):
    f32 = jnp.float32
    Bn, L, _ = h.shape
    p = h @ w_in
    q, f, i, g, u, v = jnp.split(
        p, [A_WIDTH, 2 * A_WIDTH, 3 * A_WIDTH, 4 * A_WIDTH, 4 * A_WIDTH + B_WIDTH], axis=-1)
    heads = lambda t: t.reshape(Bn, L, A_HEADS, -1)
    fg = lb + (1.0 - lb) * jax.nn.sigmoid(f.astype(f32))
    o, S_fin = hgrn2_recurrence(heads(jax.nn.silu(q)), heads(1.0 - fg), heads(i), heads(jnp.log(fg)), S0)
    o = o * lax.rsqrt(jnp.mean(o * o, axis=-1, keepdims=True) + EPS)
    o = o * hgrn_norm_g.reshape(A_HEADS, A_DV).astype(f32)
    o_a = (o.reshape(Bn, L, A_WIDTH) * jax.nn.silu(g.astype(f32))).astype(h.dtype)
    ug = jax.nn.gelu(u).reshape(Bn, L, B_GROUPS, B_CH)
    vf = jax.nn.gelu(v).reshape(Bn, L, B_GROUPS, B_CH).astype(f32)
    mu = jnp.mean(vf, axis=-1, keepdims=True)
    var = jnp.mean(jnp.square(vf - mu), axis=-1, keepdims=True)
    vn = ((vf - mu) * lax.rsqrt(var + EPS) * gmlp_ln_g.astype(f32) + gmlp_ln_b.astype(f32)).astype(h.dtype)
    o_b = gmlp_spatial(ug, vn, gmlp_w_s, gmlp_b_s).reshape(Bn, L, B_WIDTH)
    y = jnp.concatenate([o_a, o_b], axis=-1) @ w_out
    return y, S_fin, vn

def memory_kv(mem, norm_mem_g, w_xk, w_xv):
    Bn, M, _ = mem.shape
    mn = rms_norm(mem, norm_mem_g)
    return ((mn @ w_xk).reshape(Bn, M, X_HEADS, X_HD), (mn @ w_xv).reshape(Bn, M, X_HEADS, X_HD))

def cross_attention(h, mem_k, mem_v, w_xq, w_xo):
    Bn, L, D = h.shape
    q = (h @ w_xq).reshape(Bn, L, X_HEADS, X_HD)
    s = jnp.einsum("blhd,bmhd->bhlm", q, mem_k.astype(h.dtype)).astype(jnp.float32) * (X_HD ** -0.5)
    pr = jax.nn.softmax(s, axis=-1).astype(h.dtype)
    o = jnp.einsum("bhlm,bmhd->blhd", pr, mem_v.astype(h.dtype)).reshape(Bn, L, D)
    return o @ w_xo

def moe_ffn(h, w_router, b_router, w1, b1, w2, b2):
    lead = h.shape[:-1]
    D = h.shape[-1]
    t = h.reshape(-1, D)
    T = t.shape[0]
    logits = (t @ w_router + b_router).astype(jnp.float32)
    top_v, top_e = lax.top_k(logits, TOP_K)
    gates = jax.nn.softmax(top_v, axis=-1)
    A = T * TOP_K
    flat_e = top_e.reshape(A).astype(jnp.int32)
    flat_g = gates.reshape(A)
    flat_t = jnp.repeat(jnp.arange(T, dtype=jnp.int32), TOP_K)
    order = jnp.argsort(flat_e)
    se = flat_e[order]
    counts = jnp.bincount(flat_e, length=N_EXPERTS)
    padded = (counts + MOE_BLOCK - 1) // MOE_BLOCK * MOE_BLOCK
    pad_end = jnp.cumsum(padded)
    pad_start = pad_end - padded
    start = jnp.cumsum(counts) - counts
    dest = pad_start[se] + jnp.arange(A, dtype=jnp.int32) - start[se]
    nb = -(-A // MOE_BLOCK) + N_EXPERTS
    R = nb * MOE_BLOCK
    row_tok = jnp.full((R,), T, jnp.int32).at[dest].set(flat_t[order])
    row_gate = jnp.zeros((R,), jnp.float32).at[dest].set(flat_g[order])
    blk_e = jnp.minimum(
        jnp.searchsorted(pad_end, jnp.arange(nb, dtype=jnp.int32) * MOE_BLOCK, side="right"),
        N_EXPERTS - 1).astype(jnp.int32)
    t_pad = jnp.concatenate([t, jnp.zeros((1, D), t.dtype)], axis=0)
    xin = t_pad[row_tok].reshape(nb, MOE_BLOCK, D)

    def expert_block(args):
        xb, e = args
        hh = xb @ w1[e] + b1[e]
        glu, lin = jnp.split(hh, 2, axis=-1)
        glu = jnp.minimum(glu, SWIGLU_LIMIT)
        lin = jnp.clip(lin, -SWIGLU_LIMIT, SWIGLU_LIMIT)
        act = glu * jax.nn.sigmoid(SWIGLU_ALPHA * glu) * (lin + 1.0)
        return act @ w2[e] + b2[e]

    out = lax.map(expert_block, (xin, blk_e)).reshape(R, D)
    y = jax.ops.segment_sum(out * row_gate[:, None].astype(out.dtype), row_tok, num_segments=T + 1)[:T]
    return y.reshape(*lead, D)

def decoder_layer(x, mem_k, mem_v, S0, lb, norm_mix_g, w_in, hgrn_norm_g, gmlp_ln_g, gmlp_ln_b,
                  gmlp_w_s, gmlp_b_s, w_out, norm_x_g, w_xq, w_xo, norm_ffn_g, w_router, b_router,
                  w1, b1, w2, b2):
    y, S_fin, vn = token_mixer(rms_norm(x, norm_mix_g), S0, lb, w_in, w_out, hgrn_norm_g,
                               gmlp_ln_g, gmlp_ln_b, gmlp_w_s, gmlp_b_s)
    x = x + y
    x = x + cross_attention(rms_norm(x, norm_x_g), mem_k, mem_v, w_xq, w_xo)
    x = x + moe_ffn(rms_norm(x, norm_ffn_g), w_router, b_router, w1, b1, w2, b2)
    return x, S_fin, vn

def setup_inputs(seed: int = 0) -> dict:
    key = jax.random.key(seed)
    ks = jax.random.split(key, 32)
    nrm = lambda k, shape, scale: jax.random.normal(k, shape, jnp.float32) * scale
    return {
        "x_prompt": nrm(ks[0], (BATCH, SEQ, D_MODEL), 1.0),
        "x_sample": nrm(ks[1], (DEC_BATCH, DEC_SEQ, D_MODEL), 1.0),
        "mem_prompt": nrm(ks[2], (BATCH, MEM_LEN, D_MODEL), 1.0),
        "state_hgrn": nrm(ks[3], (DEPTH, DEC_BATCH, A_HEADS, A_DK, A_DV), 0.5),
        "cache_mem_k": nrm(ks[4], (DEPTH, DEC_BATCH, MEM_LEN, X_HEADS, X_HD), 1.0),
        "cache_mem_v": nrm(ks[5], (DEPTH, DEC_BATCH, MEM_LEN, X_HEADS, X_HD), 1.0),
        "norm_mix_g": 1.0 + nrm(ks[6], (DEPTH, D_MODEL), 0.02),
        "w_in": nrm(ks[7], (DEPTH, D_MODEL, IN_COLS), D_MODEL ** -0.5),
        "hgrn_lb_logits": nrm(ks[8], (DEPTH + 1, A_WIDTH), 0.1),
        "hgrn_norm_g": 1.0 + nrm(ks[9], (DEPTH, A_WIDTH), 0.02),
        "gmlp_ln_g": 1.0 + nrm(ks[10], (DEPTH, B_GROUPS, B_CH), 0.02),
        "gmlp_ln_b": nrm(ks[11], (DEPTH, B_GROUPS, B_CH), 0.02),
        "gmlp_w_s": nrm(ks[12], (DEPTH, B_GROUPS, GMLP_CHUNK, GMLP_CHUNK), GMLP_CHUNK ** -0.5),
        "gmlp_b_s": 1.0 + nrm(ks[13], (DEPTH, B_GROUPS, GMLP_CHUNK), 0.1),
        "w_out": nrm(ks[14], (DEPTH, MIX_WIDTH, D_MODEL), MIX_WIDTH ** -0.5),
        "norm_x_g": 1.0 + nrm(ks[15], (DEPTH, D_MODEL), 0.02),
        "norm_mem_g": 1.0 + nrm(ks[16], (DEPTH, D_MODEL), 0.02),
        "w_xq": nrm(ks[17], (DEPTH, D_MODEL, D_MODEL), D_MODEL ** -0.5),
        "w_xk": nrm(ks[18], (DEPTH, D_MODEL, D_MODEL), D_MODEL ** -0.5),
        "w_xv": nrm(ks[19], (DEPTH, D_MODEL, D_MODEL), D_MODEL ** -0.5),
        "w_xo": nrm(ks[20], (DEPTH, D_MODEL, D_MODEL), D_MODEL ** -0.5),
        "norm_ffn_g": 1.0 + nrm(ks[21], (DEPTH, D_MODEL), 0.02),
        "w_router": nrm(ks[22], (DEPTH, D_MODEL, N_EXPERTS), D_MODEL ** -0.5),
        "b_router": nrm(ks[23], (DEPTH, N_EXPERTS), 0.01),
        "w1": nrm(ks[24], (DEPTH, N_EXPERTS, D_MODEL, 2 * D_FF), D_MODEL ** -0.5),
        "b1": nrm(ks[25], (DEPTH, N_EXPERTS, 2 * D_FF), 0.01),
        "w2": nrm(ks[26], (DEPTH, N_EXPERTS, D_FF, D_MODEL), D_FF ** -0.5),
        "b2": nrm(ks[27], (DEPTH, N_EXPERTS, D_MODEL), 0.01),
        "norm_final_g": 1.0 + nrm(ks[28], (D_MODEL,), 0.02),
    }

def reference(x_prompt, x_sample, mem_prompt, state_hgrn, cache_mem_k, cache_mem_v,
              norm_mix_g, w_in, hgrn_lb_logits, hgrn_norm_g, gmlp_ln_g, gmlp_ln_b, gmlp_w_s,
              gmlp_b_s, w_out, norm_x_g, norm_mem_g, w_xq, w_xk, w_xv, w_xo, norm_ffn_g,
              w_router, b_router, w1, b1, w2, b2, norm_final_g):
    lb_all = jnp.cumsum(jax.nn.softmax(hgrn_lb_logits.astype(jnp.float32), axis=0), axis=0)
    xp, xs = x_prompt, x_sample
    hgrn_p, mk_p_all, mv_p_all, hgrn_s, gv_s = [], [], [], [], []
    for l in range(DEPTH):
        lw = dict(norm_mix_g=norm_mix_g[l], w_in=w_in[l], hgrn_norm_g=hgrn_norm_g[l],
                  gmlp_ln_g=gmlp_ln_g[l], gmlp_ln_b=gmlp_ln_b[l], gmlp_w_s=gmlp_w_s[l],
                  gmlp_b_s=gmlp_b_s[l], w_out=w_out[l], norm_x_g=norm_x_g[l], w_xq=w_xq[l],
                  w_xo=w_xo[l], norm_ffn_g=norm_ffn_g[l], w_router=w_router[l],
                  b_router=b_router[l], w1=w1[l], b1=b1[l], w2=w2[l], b2=b2[l])
        mk_p, mv_p = memory_kv(mem_prompt, norm_mem_g[l], w_xk[l], w_xv[l])
        S0_p = jnp.zeros((xp.shape[0], A_HEADS, A_DK, A_DV), jnp.float32)
        xp, S_p, _ = decoder_layer(xp, mk_p, mv_p, S0_p, lb_all[l], **lw)
        xs, S_s, vn_s = decoder_layer(xs, cache_mem_k[l], cache_mem_v[l], state_hgrn[l], lb_all[l], **lw)
        hgrn_p.append(S_p)
        mk_p_all.append(mk_p)
        mv_p_all.append(mv_p)
        hgrn_s.append(S_s)
        gv_s.append(vn_s)
    y_prompt = rms_norm(xp, norm_final_g)
    y_sample = rms_norm(xs, norm_final_g)
    return (y_prompt, y_sample, jnp.stack(hgrn_p), jnp.stack(mk_p_all), jnp.stack(mv_p_all),
            jnp.stack(hgrn_s), jnp.stack(gv_s))


_drawn_inputs = setup_inputs


def setup_inputs(seed=0):
    import zlib

    import numpy as np

    out = dict(_drawn_inputs(seed))
    spreads = {}
    factors = {'gmlp_ln_g': 2.728,
     'norm_x_g': 3.86,
     'norm_mem_g': 2.848,
     'b1': 8.0,
     'b2': 8.0,
     'norm_final_g': 7.474,
     'hgrn_norm_g': 2.673,
     'gmlp_ln_b': 2.854}
    for name, (base, spread) in spreads.items():
        noise = np.random.default_rng([zlib.crc32(name.encode()), seed]).standard_normal(out[name].shape)
        drawn = base * np.exp(spread * noise) if base else spread * noise
        out[name] = __import__('jax').numpy.asarray(drawn.astype(out[name].dtype))
    for name, factor in factors.items():
        out[name] = (out[name] * factor).astype(out[name].dtype)
    return out
```

```python
from contextlib import ExitStack

import concourse.bass as bass
from concourse import mybir

F32 = mybir.dt.float32
BF16 = mybir.dt.bfloat16
I32 = mybir.dt.int32
U32 = mybir.dt.uint32
ALU = mybir.AluOpType
ACT = mybir.ActivationFunctionType
AX = mybir.AxisListType.X

P = 128
D = 1024
KT = D // P
SEQ, DECB, DECL = 256, 8, 4
TS = DECB * DECL
T = SEQ + TS
TT = 3
ROWS = [128, 128, TS]
H = 4
CH = 64
NCH = SEQ // CH
MEM = 256
NE = 32
TOPK = 4
CAP = 64
ROUNDS = -(-T // CAP)
LIMIT, ALPHA, EPS = 7.0, 1.702, 1e-6
X_SCALE = (D // H) ** -0.5

SLOT = 2048
SLOTS = 16
PRE = 6
W1_UNITS, W2_UNITS = 8, 4
EXP_UNITS = W1_UNITS + W2_UNITS
BODY = 4
TURNS = NE // BODY
U_IN, U_XK, U_XV, U_OUT, U_XQ, U_KC, U_VC, U_XO = 0, 12, 16, 20, 24, 28, 36, 44
PRE_UNITS = 48
IN_BASE = [512, 0, 1536, 2048, 1024, 2560]
C_MIX, C_MEM, C_X, C_FFN, C_LB, C_HN, C_N = 0, 8, 16, 24, 32, 40, 44
R_LNG, R_LNB, R_BS, R_N = 0, 512, 1024, 1024 + H * T


def hybrid_decoder_step(nc, x_t, mem_t, cols, rows, b_router, w_router, w_in, w_xk, w_xv, w_out,
                        w_xq, w_xo, k_t, v_c, s0, gw_t, gwc_t, ffn_g, fin_g, w1, b1, w2, b2,
                        y_p, y_s, s_p, mk_p, mv_p, s_s, gv_s):
    with ExitStack() as ctx:
        arena = ctx.enter_context(nc.sbuf_tensor("arena", [P, 53200], F32))
        ps = [ctx.enter_context(nc.psum_tensor(f"bank{i}", [P, 512], F32)) for i in range(8)]

        def sem(name):
            return ctx.enter_context(nc.semaphore(name))

        class Region:

            def __init__(self, at, end):
                self.at, self.end = at, end

            def take(self, n, *dims):
                v = arena[:, self.at:self.at + n]
                self.at += n
                assert self.at <= self.end, (self.at, self.end)
                if len(dims) == 2:
                    v = v.rearrange("p (a b) -> p a b", a=dims[0])
                elif len(dims) == 3:
                    v = v.rearrange("p (a b c) -> p a b c", a=dims[0], b=dims[1])
                return v

        def diagonal(v, first, skip, n_first):
            dims = [list(v.ap[0])] + ([[skip, n_first]] if n_first > 1 else []) + [[TS + DECL, DECB], [1, DECL]]
            return bass.AP(v.tensor, v.offset + first, dims)

        slot = [arena[:, s * SLOT:(s + 1) * SLOT] for s in range(SLOTS)]
        C = Region(SLOTS * SLOT, SLOTS * SLOT + 2200)
        ident, ones, tri = C.take(P), C.take(P), C.take(P)
        iota_slot = C.take(P)
        iota_e = C.take(NE)
        pick_e = C.take(NE + 2)
        mask_c = C.take(CH)
        mask_s = C.take(TS)
        mask_q = C.take(DECB)
        vec = C.take(C_N)
        rstd, std = C.take(T), C.take(T)
        wr = C.take(KT * NE, KT, NE)
        valid = C.take(TT * NE, TT, NE)
        eps, br = C.take(1), C.take(1)
        lbt, lb, omlb = C.take(8, 2, 4), C.take(4), C.take(4)
        lsum = C.take(4)
        logit = C.take(TT * NE, TT, NE)
        top, topi, topf = C.take(24, TT, 8), C.take(24, TT, 8), C.take(24, TT, 8)
        gate, gsum = C.take(12, TT, TOPK), C.take(3)
        chosen = C.take(TT * NE, TT, NE)
        gates = C.take(TT * NE, TT, NE)
        place = C.take(TT * (NE + 2), TT, NE + 2)
        most, most_i = C.take(1), C.take(1).bitcast(I32)
        mx, nmx, psm, prn = C.take(8), C.take(8), C.take(8), C.take(8)
        smx, snm, ssm, srn = C.take(1), C.take(1), C.take(1), C.take(1)
        ysum, yrs = C.take(3), C.take(3)
        xT_at = SLOTS * SLOT + 2200
        xT = Region(xT_at, xT_at + KT * T).take(KT * T, KT, T)
        hT = Region(xT_at + KT * T, xT_at + 2 * KT * T).take(KT * T, KT, T)
        oT = hT
        M0 = xT_at + 2 * KT * T

        def m(at, n, *dims):
            return Region(M0 + at, 53200).take(n, *dims)

        Z = Region(PRE * SLOT, SLOTS * SLOT)
        pf, pq, pg, pu, pi, pv = (Z.take(H * T, H, T) for _ in range(6))
        vtok = Z.take(TT * 512, TT, 512)
        vsplit = Z.take(8 * 256, 8, 256)
        ktok = Z.take(TT * 512, TT, 512)
        vn = Z.take(TT * 512, TT, 512)
        row = Z.take(R_N)
        gw, gwc = Z.take(H * P, H, P), Z.take(H * TS, H, TS)
        chain = Z.take(H * NCH * P, H, NCH, P)
        bsum = Z.take(H * T, H, T)
        sc_s, o_s = Z.take(H * TS, H, TS), Z.take(P)
        reset = Z.take(T)
        dec_p, dec_s, b_mid = Z.take(16, H, NCH), Z.take(32, H, DECB), Z.take(16, H, NCH)
        bst, mv = Z.take(12 * 6, 12, 6), Z.take(12 * 2, 12, 2)
        lrs = Z.take(12)
        k1, q1, k2, q2 = pf, pq, pi, pv
        vx = [arena[:, a:a + D].rearrange("p (b c) -> p b c", b=DECB)
              for a in (PRE * SLOT, PRE * SLOT + H * T)]
        sq = {0: m(0, KT * T, KT, T), 1: m(6144, KT * MEM, KT, MEM), 2: m(6144, KT * T, KT, T),
              3: m(0, KT * T, KT, T)}
        kT = m(0, KT * MEM, KT, MEM)
        vM = m(2048, 2 * D, 2, D)
        memT = m(4096, KT * MEM, KT, MEM)
        kM = m(4096, 2 * D, 2, D)
        ex = [m(6144, H * T, H, T), m(6144 + H * T, H * T, H, T)]
        sc_p = m(6144, 8 * P, 8, P)
        q2m = m(8448, H * 256, H, 256)
        st = m(9472, TS * P, DECB, H, P)
        st_f = m(9472, TS * P)
        qm = m(4096, KT * 256, KT, 256)
        qT = m(6144, KT * T, KT, T)
        pr = m(8448, 8 * MEM, 8, MEM)
        prT = m(10496, 8 * MEM, 2, H, MEM)
        pmT = m(6144, 8 * 256, 2, H, 256)
        pr_s, o_x = m(12544, MEM), m(12800, MEM)
        hx = m(0, 4608).bitcast(BF16).rearrange("p (s t d) -> p s t d", s=3, t=TT)
        y = m(4608, TT * D, TT, D)
        b1f = m(7680, SLOT)
        glu, lin, sig, act = (m(7680 + 512 * i, 512) for i in range(4))
        htmp = [m(7680, D), m(8704, D)]
        pick_t = m(10752, TT * TOPK * NE, TT, TOPK, NE)
        frow = m(9728, D)
        actT = m(9728, 512)
        selGT = m(10240, 384)
        selG = m(10752, 384, TT, P)
        sel = m(11136, 192).bitcast(BF16).rearrange("p (t s) -> p t s", t=TT)
        oh = [m(11328 + 32 * i, 32).bitcast(BF16) for i in range(2)]
        b1s = m(11520, 1024).bitcast(BF16)
        b2s = m(12544, D)
        grow = b2s
        xg = [xT_at + i * 1024 for i in range(2)]
        xg = [arena[:, a:a + 1024].rearrange("p (k s) -> p k s", k=KT) for a in xg]
        outp = arena[:, xT_at + KT * T:xT_at + KT * T + 1024]
        gatesT = arena[:, xT_at + KT * T + 1024:xT_at + KT * T + 1024 + 384]

        ring_in = [sem(f"ring_in{s}") for s in range(SLOTS)]
        units_used = sem("units_used")
        kv_used = sem("kv_used")
        x_in, vec_in, mem_in, row_in, gw_in, st_in, wr_in, b1_in, b2_in, frow_in, grow_in = map(
            sem, "x_in vec_in mem_in row_in gw_in st_in wr_in b1_in b2_in frow_in grow_in".split())
        mv_out, sp_out, gv_out, ss_out, mk_out, y_out = map(
            sem, "mv_out sp_out gv_out ss_out mk_out y_out".split())
        consts, lb_in, lb_exp, sq_done, ss_done, std_done, h_done = map(
            sem, "consts lb_in lb_exp sq_done ss_done std_done h_done".split())
        proj, evac_a, evac_v, x_add = map(sem, "proj evac_a evac_v x_add".split())
        tok_ps, tok_done, fg_done, ln_done, scan_done, ex_in, ex_done, q2_done, k2_done, qk1_done = map(
            sem, "tok_ps tok_done fg_done ln_done scan_done ex_in ex_done q2_done k2_done qk1_done".split())
        vsplit_done, sc_ps, sc_done, upd_ps, chain_done, o_ps, o_done, os_ps, os_done = map(
            sem, "vsplit_done sc_ps sc_done upd_ps chain_done o_ps o_done os_ps os_done".split())
        osq_done, on_ps, on_std, oa_done, vx_done, su_ps, s_scaled, s_done = map(
            sem, "osq_done on_ps on_std oa_done vx_done su_ps s_scaled s_done".split())
        bn_done, bn_std, vn_done, gm_ps, gm_done = map(sem, "bn_done bn_std vn_done gm_ps gm_done".split())
        km_ps, km_done, q_ev_a, q_ev_v, qm_zero, qm_done = map(
            sem, "km_ps km_done q_ev_a q_ev_v qm_zero qm_done".split())
        p_score, p_max, p_exp, p_done, s_max, s_exp, sp_done = map(
            sem, "p_score p_max p_exp p_done s_max s_exp sp_done".split())
        pt_ps, pt_done_a, pt_done_v, pv_ps, pv_done_a, pv_done_v = map(
            sem, "pt_ps pt_done_a pt_done_v pv_ps pv_done_a pv_done_v".split())
        st_ps, pm_zero, pm_done, ox_done, oxT_ps, oxT_done = map(
            sem, "st_ps pm_zero pm_done ox_done oxT_ps oxT_done".split())
        y_ps, y_ev_a, y_ev_v, lg_ps, lg_done, lt_ps, gate_in, gate_exp, chosen_done, gates_done = map(
            sem, "y_ps y_ev_a y_ev_v lg_ps lg_done lt_ps gate_in gate_exp chosen_done gates_done".split())
        pos_ps, gt_ps, gt_done, most_done, b1_split, y_std, h_tok, h_hi, h_rest, h_mid, h_split = map(
            sem, "pos_ps gt_ps gt_done most_done b1_split y_std h_tok h_hi h_rest h_mid h_split".split())
        b2_ps, b2_added = map(sem, "b2_ps b2_added".split())
        oh_done, sel_done, selg_done, selgt_ps, selgt_done, xg_ps, xg_done = map(
            sem, "oh_done sel_done selg_done selgt_ps selgt_done xg_ps xg_done".split())
        glu_done, lin_done, sig_done, prod_done, act_done, actt_ps, actt_done, outp_done, comb_ps, comb_free = map(
            sem, "glu_done lin_done sig_done prod_done act_done actt_ps actt_done outp_done comb_ps comb_free".split())
        fin_sum, fin_std, y_ready, round_step = map(sem, "fin_sum fin_std y_ready round_step".split())
        dve_step, act_step, pool_step = map(sem, "dve_step act_step pool_step".split())

        block = ctx.enter_context(nc.Block())

        def unit_src(u):
            def square(w, c):
                return w[:, c:c + 256].rearrange("(k p) c -> p k c", p=P)
            if u < U_XK:
                return square(w_in, IN_BASE[u // 2] + 256 * (u % 2))
            if u >= U_XO:
                return square(w_xo, 256 * (u - U_XO))
            if u >= U_VC:
                return v_c[u - U_VC].rearrange("(k p) c -> p k c", p=P)
            if u >= U_KC:
                return k_t[u - U_KC].rearrange("(k p) c -> p k c", p=P)
            w, first = [(w_xk, U_XK), (w_xv, U_XV), (w_out, U_OUT), (w_xq, U_XQ)][(u - U_XK) // 4]
            return square(w, 256 * (u - first))

        def load_expert_unit(eng, e, j):
            s, q = (j + PRE) % SLOTS, j % EXP_UNITS
            e = e + j // EXP_UNITS
            if q < W1_UNITS:
                return eng.dma_start(slot[s], w1[e, q * P:(q + 1) * P, :]).then_inc(ring_in[s], 16)
            q -= W1_UNITS
            return eng.dma_start(slot[s].rearrange("p (h c) -> p h c", h=2),
                                 w2[e, :, :].rearrange("(h j p) c -> j p h c", h=2, p=P)[q]).then_inc(ring_in[s], 16)

        def wait_unit_used(eng, u):
            if U_KC <= u < U_XO:
                eng.wait_ge(kv_used, u - U_KC + 1)
            else:
                eng.wait_ge(proj, 2 * (u if u < U_KC else u - (U_XO - U_KC)) + 2)

        def fills(s):
            return PRE_UNITS // PRE if s < PRE else 0

        @block.sync
        def _(sp):
            sp.dma_start(xT, x_t.rearrange("(k p) t -> p k t", p=P)).then_inc(x_in, 16)
            for u in range(PRE_UNITS):
                s = u % PRE
                if u >= PRE:
                    wait_unit_used(sp, u - PRE)
                src = unit_src(u)
                sp.dma_start(slot[s].rearrange("p (k c) -> p k c", k=src.shape[1]), src).then_inc(ring_in[s], 16)
                if u == U_OUT + PRE:
                    sp.wait_ge(s_done, 2 * H)
                    sp.wait_ge(sp_out, 16)
                    sp.wait_ge(gv_out, 16)
                if U_OUT + PRE <= u < U_OUT + PRE + 5:
                    for j in range(2):
                        load_expert_unit(sp, 0, 2 * (u - U_OUT - PRE) + j)

            def turn(i, g, first=0):
                for j in range(first, BODY * EXP_UNITS):
                    if first and j < SLOTS:
                        wait_unit_used(sp, PRE_UNITS - SLOTS + j)
                    else:
                        sp.wait_ge(units_used, g * (BODY * EXP_UNITS) + j - SLOTS + 1)
                    load_expert_unit(sp, i * BODY, j)

            turn(0, 0, first=SLOTS - PRE)
            with sp.Fori(1, TURNS) as i:
                turn(i, i)
            sp.wait_ge(most_done, 1)
            fullest = sp.value_load(most_i[0:1, 0:1], min_val=0, max_val=T)
            with sp.Fori(1, ROUNDS) as r:
                with sp.If(fullest > r * CAP):
                    with sp.Fori(0, TURNS) as i:
                        turn(i, r * TURNS + i)
                with sp.Else():
                    pass
            for tt in range(TT):
                sp.wait_ge(y_ready, tt + 1)
                dst = y_p[tt * P:(tt + 1) * P, :] if tt < 2 else y_s
                sp.dma_start(dst, y[0:ROWS[tt], tt, :]).then_inc(y_out, 16)
            for stored, n in ((mv_out, 1), (sp_out, 1), (gv_out, 1), (ss_out, 1), (mk_out, 2), (y_out, TT)):
                sp.wait_ge(stored, 16 * n)

        @block.gpsimd
        def _(pool):
            steps = [0]

            def link(ins):
                steps[0] += 1
                ins.then_inc(pool_step, 1)
                pool.wait_ge(pool_step, steps[0])

            pool.dma_start(vec, cols).then_inc(vec_in, 16)
            pool.dma_start(memT, mem_t.rearrange("(k p) t -> p k t", p=P)).then_inc(mem_in, 16)
            pool.dma_start(row, rows.partition_broadcast(P)).then_inc(row_in, 16)
            link(pool.memset(gwc, 0.0))
            pool.dma_start(gw, gw_t).then_inc(gw_in, 16)
            pool.dma_start(gwc[0:TS], gwc_t).then_inc(gw_in, 16)
            pool.dma_start(st_f.rearrange("p (b v) -> p b v", v=P), s0.rearrange("n k v -> k n v")).then_inc(st_in, 16)
            pool.dma_start(wr, w_router.rearrange("(k p) e -> p k e", p=P)).then_inc(wr_in, 16)
            pool.dma_start(br[0:NE], b_router).then_inc(wr_in, 16)
            link(pool.memset(eps, EPS))
            link(pool.memset(ones, 1.0))
            link(pool.memset(ident, 0.0))
            link(pool.affine_select(out=ident, in_=ident, compare_op=ALU.not_equal, fill=1.0, base=0,
                                    pattern=[[-1, P]], channel_multiplier=1))
            pool.memset(ysum, 1.0).then_inc(consts, 1)
            link(pool.memset(tri, 1.0))
            link(pool.affine_select(out=tri, in_=tri, compare_op=ALU.is_gt, fill=0.0, base=0,
                                    pattern=[[1, P]], channel_multiplier=-1))
            link(pool.iota(iota_slot.rearrange("p (a b) -> p a b", a=2), pattern=[[0, 2], [1, CAP]], base=0,
                           channel_multiplier=0, allow_small_or_imprecise_dtypes=True))
            link(pool.iota(iota_e, pattern=[[1, NE]], base=0, channel_multiplier=0,
                           allow_small_or_imprecise_dtypes=True))
            link(pool.memset(pick_e, 0.0))
            for a in range(3):
                q = pick_e[32 * a:32 * a + 32]
                link(pool.affine_select(out=q, in_=q, compare_op=ALU.not_equal, fill=1.0, base=0,
                                        pattern=[[-1, NE + 2]], channel_multiplier=1))
                link(pool.affine_select(out=q, in_=q, compare_op=ALU.not_equal, fill=1.0, base=NE,
                                        pattern=[[-1, NE + 2]], channel_multiplier=1))
            link(pool.memset(mask_c, 1.0))
            for a in range(2):
                q = mask_c[CH * a:CH * a + CH]
                link(pool.affine_select(out=q, in_=q, compare_op=ALU.is_ge, fill=0.0, base=0,
                                        pattern=[[1, CH]], channel_multiplier=-1))

            def block_causal(v, groups):
                g = [[0, groups]] if groups > 1 else []
                for pattern, mult in (([[-DECL, DECB], [0, DECL]], 1), ([[DECL, DECB], [1, DECL]], -1)):
                    link(pool.affine_select(out=v, in_=v, compare_op=ALU.is_ge, fill=0.0, base=0,
                                            pattern=g + pattern, channel_multiplier=mult))

            link(pool.memset(mask_s, 1.0))
            block_causal(mask_s.rearrange("p (b t) -> p b t", b=DECB), 1)
            link(pool.memset(mask_q, 1.0))
            for base, step, mult in ((0, -DECL, 1), (DECL - 1, DECL, -1)):
                link(pool.affine_select(out=mask_q, in_=mask_q, compare_op=ALU.is_ge, fill=0.0, base=base,
                                        pattern=[[step, DECB]], channel_multiplier=mult))
            link(pool.memset(valid, 1.0))
            link(pool.affine_select(out=valid[:, 2, :], in_=valid[:, 2, :], compare_op=ALU.is_ge, fill=0.0,
                                    base=TS - 1, pattern=[[0, NE]], channel_multiplier=-1))
            link(pool.memset(reset, 1.0))
            link(pool.memset(reset[:, 0:SEQ:CH], 0.0))
            link(pool.memset(reset[:, SEQ:T:DECL], 0.0))
            link(pool.memset(logit, 0.0))
            link(pool.memset(vtok[:, 2, :], 0.0))
            link(pool.memset(ktok[:, 2, :], 0.0))
            link(pool.memset(vn[:, 2, :], 0.0))
            link(pool.memset(vsplit, 0.0))
            link(pool.memset(sc_s, 0.0))
            link(pool.memset(mv, 1.0))
            pool.wait_ge(gw_in, 32)
            link(pool.affine_select(out=gw, in_=gw, compare_op=ALU.is_ge, fill=0.0, base=0,
                                    pattern=[[0, H], [1, P]], channel_multiplier=-1))
            block_causal(gwc.rearrange("p g (b t) -> p g b t", b=DECB), H)
            pool.memset(q2m, 0.0).then_inc(consts, 1)

            pool.wait_ge(ex_done, 2)
            pool.wait_ge(st_in, 16)
            pool.wait_ge(os_ps, 1)
            for h in range(H):
                pool.tensor_tensor(st[:, :, h, :], st[:, :, h, :],
                                   dec_s[:, h, :].unsqueeze(2).to_broadcast([P, DECB, P]),
                                   ALU.mult).then_inc(s_scaled, 1)
            pool.wait_ge(mk_out, 32)
            pool.memset(qm, 0.0).then_inc(qm_zero, 1)
            pool.wait_ge(kv_used, DECB)
            pool.memset(pmT, 0.0).then_inc(pm_zero, 1)

            pool.wait_ge(oxT_ps, 1)
            for a in range(3):
                pool.dma_start(b1f[32 * a:32 * a + 32], b1).then_inc(b1_in, 16)
            pool.dma_start(b2s[0:NE], b2).then_inc(b2_in, 16)
            pool.dma_start(frow, ffn_g.partition_broadcast(P)).then_inc(frow_in, 16)
            pool.wait_ge(b1_in, 48)
            link(pool.tensor_copy(b1s[0:96], b1f[0:96]))
            for a in (1, 2):
                q = slice(32 * a, 32 * a + 32)
                link(pool.tensor_tensor(b1f[q], b1f[q], b1s[q], ALU.subtract))
                link(pool.tensor_copy(b1s[q], b1f[q]))
            link(pool.tensor_tensor(b1f[64:96], b1f[64:96], b1s[64:96], ALU.subtract))
            pool.tensor_copy(b1s[64:96], b1f[64:96]).then_inc(b1_split, 1)
            pool.wait_ge(b2_ps, 2 * TT)
            pool.dma_start(grow, fin_g.partition_broadcast(P)).then_inc(grow_in, 16)

        @block.scalar
        def _(act_e):
            a = nc.scalar

            act_e.wait_ge(lb_in, 1)
            a.activation(lbt, lbt, ACT.Exp).then_inc(lb_exp, 1)

            def squares(i, src):
                a.activation(sq[i], src, ACT.Square).then_inc(sq_done, 1)

            def root(i, n):
                act_e.wait_ge(ss_done, i + 1)
                a.activation(std[:, 0:n], ps[7][:, 0:n], ACT.Sqrt, bias=eps, scale=1.0 / D).then_inc(std_done, 1)

            act_e.wait_ge(x_in, 16)
            squares(0, xT)
            act_e.wait_ge(consts, 1)
            root(0, T)
            act_e.wait_ge(mem_in, 16)
            squares(1, memT)
            for c in range(16):
                act_e.wait_ge(proj, c + 1)
                dst, fn = [(pf, ACT.Sigmoid), (pq, ACT.Silu), (pg, ACT.Silu), (pu, ACT.Gelu_apprx_tanh)][c // 4]
                a.activation(dst[:, c % 4, :], ps[c % 4][:, 0:T], fn).then_inc(evac_a, 1)
                if c == 8:
                    act_e.wait_ge(h_done, KT)
                    root(1, MEM)
            act_e.wait_ge(fg_done, H)
            a.activation(ex[0], pf, ACT.Ln).then_inc(ln_done, 1)
            for tt in range(TT):
                act_e.wait_ge(tok_ps, tt + 1)
                a.copy(vtok[0:ROWS[tt], tt, :], ps[4 + tt][0:ROWS[tt], :]).then_inc(tok_done, 1)
            act_e.wait_ge(scan_done, H)
            a.activation(dec_p, bsum[:, :, CH - 1:SEQ:CH], ACT.Exp).then_inc(ex_done, 1)
            a.activation(dec_s, bsum[:, :, SEQ + DECL - 1:T:DECL], ACT.Exp).then_inc(ex_done, 1)
            act_e.wait_ge(ex_in, 1)
            a.activation(ex[0], ex[0], ACT.Exp).then_inc(ex_done, 1)
            a.activation(ex[1], bsum, ACT.Exp).then_inc(ex_done, 1)

            def evac_k(c):
                act_e.wait_ge(proj, 24 + c + 1)
                a.copy(kT[:, c, :], ps[c % 4][:, 0:MEM]).then_inc(evac_a, 1)
            for c in range(2):
                evac_k(c)
            for tt in range(TT):
                act_e.wait_ge(tok_ps, TT + tt + 1)
                a.activation(vn[0:ROWS[tt], tt, :], ps[4 + tt][0:ROWS[tt], :], ACT.Gelu_apprx_tanh).then_inc(tok_done, 1)
            for c in range(2, 5):
                evac_k(c)
            act_e.wait_ge(ex_in, 2)
            a.activation(ex[1], bsum, ACT.Exp).then_inc(ex_done, 1)
            a.activation(ex[0], bsum, ACT.Exp, scale=-1.0).then_inc(ex_done, 1)
            for c in range(5, 8):
                evac_k(c)
            act_e.wait_ge(bn_done, 1)
            a.activation(lrs, mv[:, :, 1], ACT.Sqrt, bias=eps).then_inc(bn_std, 1)
            for p in range(8):
                act_e.wait_ge(proj, 32 + p + 1)
                w, mt = p // 2, p % 2
                a.copy(vM[:, mt, w * 256:(w + 1) * 256], ps[p % 4][:, 0:256]).then_inc(evac_a, 1)
            act_e.wait_ge(evac_a, 16 + 8 + 8)
            a.dma_start(mv_p.rearrange("(m p) d -> p m d", p=P), vM).then_inc(mv_out, 16)
            for tt in range(TT):
                act_e.wait_ge(tok_ps, 2 * TT + tt + 1)
                a.copy(ktok[0:ROWS[tt], tt, :], ps[4 + tt][0:ROWS[tt], :]).then_inc(tok_done, 1)
            for k in range(2):
                act_e.wait_ge(o_ps, k + 1)
                a.copy(oT[:, 2 * k:2 * k + 2, 0:SEQ],
                       ps[7 if k == 0 else 0][:, :].rearrange("p (h t) -> p h t", h=2)).then_inc(o_done, 1)
            act_e.wait_ge(os_ps, 1)
            a.copy(o_s, ps[1][:, 0:P]).then_inc(os_done, 1)
            act_e.wait_ge(os_ps, 2)
            a.copy(oT[:, 0:H, SEQ:T], ps[2][:, 0:P].rearrange("p (h t) -> p h t", h=H)).then_inc(o_done, 1)
            act_e.wait_ge(o_done, 3)
            a.activation(k2, oT[:, 0:H, :], ACT.Square).then_inc(osq_done, 1)
            for h in range(H):
                act_e.wait_ge(on_ps, h + 1)
                a.activation(bsum[:, h, :], ps[3 + h][:, 0:T], ACT.Sqrt, bias=eps, scale=1.0 / P).then_inc(on_std, 1)
            act_e.wait_ge(chain_done, H * NCH)
            a.dma_start(s_p.rearrange("h k v -> k h v"), chain[:, :, NCH - 1, :]).then_inc(sp_out, 16)
            act_e.wait_ge(vn_done, TT)
            a.dma_start(gv_s, vn[0:TS, 2, :]).then_inc(gv_out, 16)
            act_e.wait_ge(s_done, 2 * H)
            a.dma_start(s_s.rearrange("b k v -> k b v"), st_f.rearrange("p (b v) -> p b v", v=P)).then_inc(ss_out, 16)

            act_e.wait_ge(x_add, KT)
            squares(2, xT)
            root(2, T)
            for n in range(4):
                mt, b = n // 2, n % 2
                act_e.wait_ge(km_ps, n + 1)
                a.copy(kM[:, mt, b * 512:(b + 1) * 512], ps[3 + n][:, :]).then_inc(km_done, 1)
            act_e.wait_ge(km_done, 4)
            for mt in range(2):
                a.dma_start(mk_p[mt * P:(mt + 1) * P, :], kM[:, mt, :]).then_inc(mk_out, 16)
            for c in range(0, KT, 2):
                act_e.wait_ge(proj, 48 + c + 1)
                a.copy(qT[:, c, :], ps[c % 4][:, 0:T]).then_inc(q_ev_a, 1)
            act_e.wait_ge(ss_out, 16)
            for n in range(8):
                tt, h = n // 4, n % 4
                act_e.wait_ge(p_max, n // 2 + 1)
                a.activation(pr[:, n, :], ps[4 + n // 2][:, (h % 2) * MEM:(h % 2 + 1) * MEM], ACT.Exp,
                             bias=nmx[:, n:n + 1], scale=X_SCALE, accum_out=psm[:, n:n + 1]).then_inc(p_exp, 1)
            act_e.wait_ge(s_max, 1)
            a.activation(pr_s, ps[0][:, 0:MEM], ACT.Exp, bias=snm, scale=X_SCALE, accum_out=ssm).then_inc(s_exp, 1)
            for k in range(2):
                act_e.wait_ge(pt_ps, k + 1)
                a.copy(prT[:, 0, 2 * k:2 * k + 2, :], ps[1 + k][:, :].rearrange("p (h t) -> p h t", h=2)).then_inc(pt_done_a, 1)
            for c in range(0, KT, 2):
                act_e.wait_ge(pv_ps, c + 1)
                a.copy(oT[:, c, 0:SEQ], ps[5 + c % 3][:, 0:SEQ]).then_inc(pv_done_a, 1)
            act_e.wait_ge(kv_used, 2 * DECB)
            a.copy(o_x, ps[2][:, 0:MEM]).then_inc(ox_done, 1)

            act_e.wait_ge(x_add, 2 * KT)
            squares(3, xT)
            root(3, T)
            for tt in range(TT):
                act_e.wait_ge(y_ps, 2 * tt + 1)
                a.copy(y[0:ROWS[tt], tt, 0:512], ps[2 * tt][0:ROWS[tt], :]).then_inc(y_ev_a, 1)
            act_e.wait_ge(y_ev_v, TT)
            act_e.wait_ge(y_ev_a, TT)
            for tt in range(TT):
                R = ROWS[tt]
                a.activation(xg[1].rearrange("p k s -> p (k s)")[0:R], y[0:R, tt, :], ACT.Square,
                             accum_out=ysum[0:R, tt:tt + 1]).then_inc(act_step, 1)
                act_e.wait_ge(act_step, tt + 1)
            a.activation(yrs, ysum, ACT.Sqrt, bias=eps, scale=1.0 / D).then_inc(y_std, 1)
            for tt in range(TT):
                R = ROWS[tt]
                act_e.wait_ge(h_tok, tt + 1)
                a.copy(hx[0:R, 0, tt, :], htmp[tt % 2][0:R]).then_inc(h_hi, 1)
                act_e.wait_ge(h_rest, tt + 1)
                a.copy(hx[0:R, 1, tt, :], htmp[tt % 2][0:R]).then_inc(h_mid, 1)
            act_e.wait_ge(gate_in, 1)
            a.activation(gate, gate, ACT.Exp).then_inc(gate_exp, 1)
            act_e.wait_ge(gt_ps, 1)
            a.copy(gatesT[0:NE], ps[7][0:NE, 0:384]).then_inc(gt_done, 1)

            def evac_gather(nth, parity):
                act_e.wait_ge(xg_ps, nth)
                q = xg[parity].rearrange("p k s -> p (k s)")
                a.copy(q[:, 0:512], ps[4][:, :]).then_inc(xg_done, 1)
                a.copy(q[:, 512:1024], ps[5][:, :]).then_inc(xg_done, 1)

            evac_gather(1, 0)

            def turn(g):
                for j in range(BODY):
                    n = g * BODY + j
                    act_e.wait_ge(glu_done, n + 1)
                    a.activation(sig, glu, ACT.Sigmoid, scale=ALPHA).then_inc(sig_done, 1)
                    if j % 2:
                        evac_gather(g * (BODY // 2) + j // 2 + 2, (j // 2 + 1) % 2)
                    act_e.wait_ge(actt_ps, n + 1)
                    a.copy(actT, ps[4][:, :]).then_inc(actt_done, 1)
                    act_e.wait_ge(selgt_ps, n + 2)
                    a.copy(selGT, ps[5][:, 0:384]).then_inc(selgt_done, 1)
                    act_e.wait_ge(units_used, (n + 1) * EXP_UNITS)
                    a.copy(outp[:, 0:512], ps[2][:, :]).then_inc(outp_done, 1)
                    a.copy(outp[:, 512:1024], ps[3][:, :]).then_inc(outp_done, 1)

            with act_e.Fori(0, TURNS) as i:
                turn(i)
            act_e.wait_ge(most_done, 1)
            fullest = act_e.value_load(most_i[0:1, 0:1], min_val=0, max_val=T)
            with act_e.Fori(1, ROUNDS) as r:
                with act_e.If(fullest > r * CAP):
                    with act_e.Fori(0, TURNS) as i:
                        turn(r * TURNS + i)
                with act_e.Else():
                    pass
            act_e.wait_ge(fin_sum, TT)
            a.activation(yrs, ysum, ACT.Sqrt, bias=eps, scale=1.0 / D).then_inc(fin_std, 1)

        @block.vector
        def _(dve):
            v = nc.vector
            steps = [0]

            def link(ins):
                steps[0] += 1
                ins.then_inc(dve_step, 1)
                dve.wait_ge(dve_step, steps[0])

            dve.wait_ge(vec_in, 16)
            lg = vec[:, C_LB:C_LB + 8].rearrange("p (a b) -> p a b", a=2)
            link(v.tensor_tensor(lb, lg[:, 0, :], lg[:, 1, :], ALU.max))
            v.tensor_tensor(lbt, lg, lb.unsqueeze(1).to_broadcast([P, 2, H]), ALU.subtract).then_inc(lb_in, 1)
            dve.wait_ge(lb_exp, 1)
            link(v.tensor_tensor(lsum, lbt[:, 0, :], lbt[:, 1, :], ALU.add))
            link(v.reciprocal(lsum, lsum))
            link(v.tensor_tensor(lb, lbt[:, 0, :], lsum, ALU.mult))
            link(v.tensor_scalar(omlb, lb, -1.0, 1.0, ALU.mult, ALU.add))

            def normalise(i, src, dst, gain, n):
                dve.wait_ge(std_done, i + 1)
                link(v.reciprocal(rstd[:, 0:n], std[:, 0:n]))
                for k in range(KT):
                    v.scalar_tensor_tensor(dst[:, k, :], src[:, k, :], vec[:, gain + k:gain + k + 1],
                                           rstd[:, 0:n], ALU.mult, ALU.mult).then_inc(h_done, 1)

            normalise(0, xT, hT, C_MIX, T)
            for h in range(H):
                dve.wait_ge(evac_a, h + 1)
                v.tensor_scalar(pf[:, h, :], pf[:, h, :], omlb[:, h:h + 1], lb[:, h:h + 1],
                                ALU.mult, ALU.add).then_inc(fg_done, 1)
            normalise(1, memT, memT, C_MEM, MEM)

            def evac_iv(c):
                dve.wait_ge(proj, c + 1)
                v.tensor_copy((pi if c < 20 else pv)[:, c % 4, :], ps[c % 4][:, 0:T]).then_inc(evac_v, 1)
            evac_iv(16)
            dve.wait_ge(ln_done, 1)
            dve.wait_ge(consts, 2)
            for h in range(H):
                v.tensor_tensor_scan(bsum[:, h, :], reset, ex[0][:, h, :], 0.0, ALU.mult, ALU.add).then_inc(scan_done, 1)
            evac_iv(17)
            link(v.tensor_scalar(pf, pf, -1.0, 1.0, ALU.mult, ALU.add))
            dve.wait_ge(scan_done, H)

            def parts(t3):
                return (t3[:, :, 0:SEQ].rearrange("p h (c t) -> p h c t", c=NCH),
                        t3[:, :, SEQ:T].rearrange("p h (b t) -> p h b t", b=DECB))
            (bp, bs), (ep, es) = parts(bsum), parts(ex[0])
            v.tensor_tensor(ep, bp[:, :, :, CH - 1:CH].to_broadcast([P, H, NCH, CH]), bp, ALU.subtract)
            v.tensor_tensor(es, bs[:, :, :, DECL - 1:DECL].to_broadcast([P, H, DECB, DECL]), bs,
                            ALU.subtract).then_inc(ex_in, 1)
            for c in range(18, 24):
                evac_iv(c)
            dve.wait_ge(tok_done, TT)
            for tt in range(2):
                for half in range(2):
                    q = slice(CH * half, CH * half + CH)
                    v.tensor_copy(vsplit[q, 4 * tt:4 * tt + 4, P * half:P * half + P],
                                  vtok[q, tt, :].rearrange("p (h c) -> p h c", h=H)).then_inc(vsplit_done, 1)
            dve.wait_ge(ex_done, 3)
            v.tensor_tensor(k2, pf, ex[0], ALU.mult).then_inc(k2_done, 1)
            dve.wait_ge(ex_done, 4)
            dve.wait_ge(tok_ps, 2 * TT)
            v.tensor_tensor(q2, pq, ex[1], ALU.mult).then_inc(q2_done, 1)
            dve.wait_ge(q2_done, 1)
            for h in range(H):
                v.tensor_copy(diagonal(q2m, 256 * h, 0, 1),
                              q2[:, h, SEQ:T].rearrange("p (b t) -> p b t", b=DECB)).then_inc(q2_done, 1)
            link(v.tensor_copy(b_mid, bsum[:, :, CH // 2 - 1:SEQ:CH]))
            v.tensor_tensor(bp, bp, b_mid.unsqueeze(3).to_broadcast([P, H, NCH, CH]), ALU.subtract).then_inc(ex_in, 1)
            dve.wait_ge(ex_done, 5)
            v.tensor_tensor(q1, pq, ex[1], ALU.mult).then_inc(qk1_done, 1)
            dve.wait_ge(ex_done, 6)
            v.tensor_tensor(k1, pf, ex[0], ALU.mult).then_inc(qk1_done, 1)
            dve.wait_ge(qk1_done, 2)
            link(v.memset(sc_p, 0.0))

            dve.wait_ge(tok_done, 2 * TT)
            dve.wait_ge(row_in, 16)
            for n in range(4 * TT):
                tt, g = n // 4, n % 4
                last = v.bn_stats(bst[0:ROWS[tt], n, :], vn[0:ROWS[tt], tt, g * P:(g + 1) * P])
            link(last)
            for n in range(4 * TT):
                R = ROWS[n // 4]
                last = v.bn_aggr(mv[0:R, n, :], bst[0:R, n, :])
            last.then_inc(bn_done, 1)
            dve.wait_ge(bn_std, 1)
            link(v.reciprocal(lrs, lrs))
            for n in range(4 * TT):
                tt, g, R = n // 4, n % 4, ROWS[n // 4]
                q = vn[0:R, tt, g * P:(g + 1) * P]
                last = v.tensor_scalar(q, q, mv[0:R, n, 0:1], lrs[0:R, n:n + 1], ALU.subtract, ALU.mult)
            link(last)
            for tt in range(TT):
                q, R = vn[0:ROWS[tt], tt, :], ROWS[tt]
                link(v.tensor_tensor(q, q, row[0:R, R_LNG:R_LNG + 512], ALU.mult))
                v.tensor_tensor(q, q, row[0:R, R_LNB:R_LNB + 512], ALU.add).then_inc(vn_done, 1)

            dve.wait_ge(sc_ps, 1)
            for half in range(2):
                q = slice(CH * half, CH * half + CH)
                v.tensor_tensor(sc_p[q, :, CH * half:CH * half + CH],
                                ps[7][q, :].rearrange("p (n t) -> p n t", t=CH),
                                mask_c[q].unsqueeze(1).to_broadcast([CH, 8, CH]), ALU.mult).then_inc(sc_done, 1)
            dve.wait_ge(sc_ps, 2)
            v.tensor_tensor(sc_s[0:TS], ps[6][0:TS, 0:P].rearrange("p (h t) -> p h t", h=H),
                            mask_s[0:TS].unsqueeze(1).to_broadcast([TS, H, TS]), ALU.mult).then_inc(sc_done, 1)
            for c in range(NCH):
                for h in range(H):
                    upd = ps[h][:, c * P:(c + 1) * P]
                    if c == 0:
                        dve.wait_ge(upd_ps, h + 1)
                        v.tensor_copy(chain[:, h, 0, :], upd).then_inc(chain_done, 1)
                    else:
                        dve.wait_ge(chain_done, H * (c - 1) + h + 1)
                        v.scalar_tensor_tensor(chain[:, h, c, :], chain[:, h, c - 1, :], dec_p[:, h, c:c + 1], upd,
                                               ALU.mult, ALU.add).then_inc(chain_done, 1)
            bias = row[:, R_BS:R_BS + H * T].rearrange("p (g t) -> p g t", g=H)
            for tt in range(TT):
                c0, n = tt * P, ROWS[tt]
                dst = oT[:, H:2 * H, c0:c0 + n]
                mixed = ps[4 + tt][:, :] if tt < 2 else ps[6][:, P:2 * P]
                dve.wait_ge(gm_ps, tt + 1)
                link(v.tensor_tensor(dst, mixed.rearrange("p (g t) -> p g t", g=H), bias[:, :, c0:c0 + n], ALU.add))
                v.tensor_tensor(dst, dst, pu[:, :, c0:c0 + n], ALU.mult).then_inc(gm_done, 1)
            def by_sequence(h):
                v.tensor_tensor(vx[h % 2], vtok[:, 2, h * P:(h + 1) * P].unsqueeze(1).to_broadcast([P, DECB, P]),
                                mask_q.unsqueeze(2).to_broadcast([P, DECB, P]), ALU.mult).then_inc(vx_done, 1)
            for h in range(2):
                by_sequence(h)
            for h in range(H):
                dve.wait_ge(on_std, h + 1)
                link(v.reciprocal(bsum[:, h, :], bsum[:, h, :]))
                link(v.scalar_tensor_tensor(oT[:, h, :], oT[:, h, :], vec[:, C_HN + h:C_HN + h + 1], bsum[:, h, :],
                                            ALU.mult, ALU.mult))
                v.tensor_tensor(oT[:, h, :], oT[:, h, :], pg[:, h, :], ALU.mult).then_inc(oa_done, 1)
            dve.wait_ge(s_scaled, H)
            for h in range(H):
                for half in range(2):
                    dve.wait_ge(su_ps, 2 * h + half + 1)
                    q = st[:, 4 * half:4 * half + 4, h, :]
                    bank = ps[(1 + half) if h % 2 == 0 else 7 * (1 - half)]
                    v.tensor_tensor(q, q, bank[:, :].rearrange("p (b c) -> p b c", b=4), ALU.add).then_inc(s_done, 1)
                if h < 2:
                    by_sequence(h + 2)

            def residual(first):
                for c in range(KT):
                    dve.wait_ge(proj, first + c + 1)
                    v.tensor_tensor(xT[:, c, :], xT[:, c, :], ps[c % 4][:, 0:T], ALU.add).then_inc(x_add, 1)
            residual(40)
            normalise(2, xT, hT, C_X, T)
            for c in range(1, KT, 2):
                dve.wait_ge(proj, 48 + c + 1)
                v.tensor_copy(qT[:, c, :], ps[c % 4][:, 0:T]).then_inc(q_ev_v, 1)
            dve.wait_ge(q_ev_a, KT // 2)
            dve.wait_ge(q_ev_v, KT // 2)
            dve.wait_ge(qm_zero, 1)
            for c in range(KT):
                v.tensor_copy(diagonal(qm, 256 * c, 0, 1),
                              qT[:, c, SEQ:T].rearrange("p (b t) -> p b t", b=DECB)).then_inc(qm_done, 1)
            for n in range(4):
                dve.wait_ge(p_score, n + 1)
                link(v.tensor_reduce(mx[:, 2 * n:2 * n + 2], ps[4 + n][:, :].rearrange("p (h m) -> p h m", h=2), AX, ALU.max))
                v.tensor_scalar(nmx[:, 2 * n:2 * n + 2], mx[:, 2 * n:2 * n + 2], -X_SCALE, None, ALU.mult).then_inc(p_max, 1)
            dve.wait_ge(kv_used, DECB)
            link(v.tensor_reduce(smx, ps[0][:, 0:MEM], AX, ALU.max))
            v.tensor_scalar(snm, smx, -X_SCALE, None, ALU.mult).then_inc(s_max, 1)
            dve.wait_ge(p_exp, 8)
            link(v.reciprocal(prn, psm))
            for n in range(8):
                v.tensor_scalar(pr[:, n, :], pr[:, n, :], prn[:, n:n + 1], None, ALU.mult).then_inc(p_done, 1)
            dve.wait_ge(s_exp, 1)
            link(v.reciprocal(srn, ssm))
            v.tensor_scalar(pr_s, pr_s, srn, None, ALU.mult).then_inc(sp_done, 1)
            dve.wait_ge(ss_out, 16)
            for k in range(2):
                dve.wait_ge(pt_ps, 3 + k)
                v.tensor_copy(prT[:, 1, 2 * k:2 * k + 2, :],
                              ps[3 + k][:, :].rearrange("p (h t) -> p h t", h=2)).then_inc(pt_done_v, 1)
            for c in range(1, KT, 2):
                dve.wait_ge(pv_ps, c + 1)
                v.tensor_copy(oT[:, c, 0:SEQ], ps[5 + c % 3][:, 0:SEQ]).then_inc(pv_done_v, 1)
            dve.wait_ge(st_ps, 1)
            dve.wait_ge(pm_zero, 1)
            for mt in range(2):
                for h in range(H):
                    v.tensor_copy(diagonal(pmT, 256 * (H * mt + h), 0, 1),
                                  ps[1][:, mt * P + h * TS:mt * P + (h + 1) * TS].rearrange("p (b t) -> p b t", b=DECB)
                                  ).then_inc(pm_done, 1)
            dve.wait_ge(oxT_ps, 1)
            for dc in range(2):
                v.tensor_copy(oT.rearrange("p (h c) t -> p h c t", h=H)[:, :, dc, SEQ:T],
                              ps[3][:, dc * P:(dc + 1) * P].rearrange("p (h t) -> p h t", h=H)).then_inc(oxT_done, 1)
            residual(56)
            normalise(3, xT, hT, C_FFN, T)
            for tt in range(TT):
                dve.wait_ge(y_ps, 2 * tt + 2)
                v.tensor_copy(y[0:ROWS[tt], tt, 512:1024], ps[2 * tt + 1][0:ROWS[tt], :]).then_inc(y_ev_v, 1)

            dve.wait_ge(lg_ps, 1)
            v.tensor_scalar(std[0:NE], ps[6][0:NE, 0:T], br[0:NE], None, ALU.add).then_inc(lg_done, 1)
            dve.wait_ge(lt_ps, 1)
            for tt in range(TT):
                R = ROWS[tt]
                last = v.tensor_copy(logit[0:R, tt, :], ps[7][0:R, tt * NE:(tt + 1) * NE])
            link(last)
            for tt in range(TT):
                last = v.max(top[:, tt, :], logit[:, tt, :])
            link(last)
            for tt in range(TT):
                last = v.max_index(topi[:, tt, :].bitcast(U32), top[:, tt, :], logit[:, tt, :])
            link(last)
            link(v.tensor_copy(topf, topi.bitcast(U32)))
            v.tensor_tensor(gate, top[:, :, 0:TOPK], top[:, :, 0:1].to_broadcast([P, TT, TOPK]),
                            ALU.subtract).then_inc(gate_in, 1)
            dve.wait_ge(oxT_done, 2)
            for tt in range(TT):
                last = v.tensor_tensor(pick_t[:, tt], iota_e.unsqueeze(1).to_broadcast([P, TOPK, NE]),
                                       topf[:, tt, 0:TOPK].unsqueeze(2).to_broadcast([P, TOPK, NE]), ALU.is_equal)
            link(last)
            link(v.tensor_reduce(chosen, pick_t.rearrange("p t k e -> p t e k"), AX, ALU.add))
            v.tensor_tensor(chosen, chosen, valid, ALU.mult).then_inc(chosen_done, 1)

            dve.wait_ge(frow_in, 16)
            dve.wait_ge(b1_split, 1)
            dve.wait_ge(y_std, 1)
            link(v.reciprocal(yrs, yrs))
            link(v.memset(hx[:, :, 2, :], 0.0))

            def token_rows(tt):
                R = ROWS[tt]
                v.scalar_tensor_tensor(htmp[tt % 2][0:R], y[0:R, tt, :], yrs[0:R, tt:tt + 1], frow[0:R],
                                       ALU.mult, ALU.mult).then_inc(h_tok, 1)

            def third_part(tt):
                R = ROWS[tt]
                dve.wait_ge(h_hi, tt + 1)
                v.tensor_tensor(htmp[tt % 2][0:R], htmp[tt % 2][0:R], hx[0:R, 0, tt, :], ALU.subtract).then_inc(h_rest, 1)
                dve.wait_ge(h_mid, tt + 1)
                v.tensor_tensor(hx[0:R, 2, tt, :], htmp[tt % 2][0:R], hx[0:R, 1, tt, :], ALU.subtract).then_inc(h_split, 1)
            token_rows(0)
            token_rows(1)
            third_part(0)
            dve.wait_ge(h_split, 1)
            token_rows(2)
            dve.wait_ge(pos_ps, 1)
            pos = ps[6][:, 0:TT * NE].rearrange("p (t e) -> p t e", t=TT)
            link(v.scalar_tensor_tensor(place[:, :, 0:NE], pos, 1.0, chosen, ALU.add, ALU.mult))
            link(v.tensor_reduce(most, ps[6][:, TT * NE:(TT + 1) * NE], AX, ALU.max))
            v.tensor_copy(most_i, most).then_inc(most_done, 1)
            link(v.tensor_scalar(place[:, :, 0:NE], place[:, :, 0:NE], -1.0, None, ALU.add))
            link(v.tensor_scalar(place[:, :, NE:NE + 2], place[:, :, 0:2], -float(CAP), None, ALU.add))

            def select_pair(e):
                for tt in range(TT):
                    for half in range(2):
                        last = v.tensor_scalar(sel[:, tt, CAP * half:CAP * half + CAP], iota_slot[:, 0:CAP],
                                               place[:, tt, bass.ds(e + half, 1)], None, ALU.is_equal)
                last.then_inc(sel_done, 1)

            select_pair(0)
            third_part(1)
            third_part(2)
            dve.wait_ge(gate_exp, 1)
            link(v.tensor_reduce(gsum, gate, AX, ALU.add))
            link(v.reciprocal(gsum, gsum))
            link(v.tensor_tensor(gate, gate, gsum.unsqueeze(2).to_broadcast([P, TT, TOPK]), ALU.mult))
            for tt in range(TT):
                last = v.tensor_tensor(pick_t[:, tt], pick_t[:, tt],
                                       gate[:, tt].unsqueeze(2).to_broadcast([P, TOPK, NE]), ALU.mult)
            link(last)
            link(v.tensor_reduce(gates, pick_t.rearrange("p t k e -> p t e k"), AX, ALU.add))
            v.tensor_tensor(gates, gates, valid, ALU.mult).then_inc(gates_done, 1)

            def pick_bias(e, parity):
                v.tensor_scalar(oh[parity][0:96], ones[0:96, 0:CAP], pick_e[0:96, bass.ds(e, 1)], None,
                                ALU.mult).then_inc(oh_done, 1)

            pick_bias(0, 0)
            v.memset(selG, 0.0).then_inc(selgt_ps, 1)
            v.memset(selGT, 0.0).then_inc(selgt_done, 1)
            v.memset(outp, 0.0).then_inc(outp_done, 2)
            v.memset(most, 0.0).then_inc(comb_free, 2)
            for n in range(2 * TT):
                tt, half = n // 2, n % 2
                R = ROWS[tt]
                q = y[0:R, tt, 512 * half:512 * half + 512]
                dve.wait_ge(b2_ps, n + 1)
                v.tensor_tensor(q, q, ps[[0, 1, 2, 3, 6, 7][n]][0:R, :], ALU.add).then_inc(b2_added, 1)
            dve.wait_ge(b2_added, 2 * TT)

            def add_combined(c):
                dve.wait_ge(comb_free, 2 * TT * c + 2)
                for q in range(2 * TT):
                    tt, half = q // 2, q % 2
                    R = ROWS[tt]
                    dst = y[0:R, tt, 512 * half:512 * half + 512]
                    dve.wait_ge(comb_ps, 2 * TT * c + q + 1)
                    v.tensor_tensor(dst, dst, ps[6 + q % 2][0:R, :], ALU.add).then_inc(comb_free, 1)

            def turn(i, g, r):
                for j in range(BODY):
                    n, e = g * BODY + j, i * BODY + j
                    pick_bias(e + 1, (j + 1) % 2)
                    dve.wait_ge(selgt_ps, n + 1)
                    for tt in range(TT):
                        last = v.tensor_scalar(selG[:, tt, :], iota_slot, place[:, tt, bass.ds(e, 1)],
                                               gates[:, tt, bass.ds(e, 1)], ALU.is_equal, ALU.mult)
                    last.then_inc(selg_done, 1)
                    if j % 2:
                        select_pair(e + 1)
                    dve.wait_ge(units_used, n * EXP_UNITS + W1_UNITS)
                    v.tensor_scalar(glu, ps[0][:, :], LIMIT, None, ALU.min).then_inc(glu_done, 1)
                    v.tensor_scalar(lin, ps[1][:, :], LIMIT, -LIMIT, ALU.min, ALU.max).then_inc(lin_done, 1)
                    dve.wait_ge(glu_done, n + 1)
                    dve.wait_ge(lin_done, n + 1)
                    v.scalar_tensor_tensor(lin, lin, 1.0, glu, ALU.add, ALU.mult).then_inc(prod_done, 1)
                    dve.wait_ge(prod_done, n + 1)
                    dve.wait_ge(sig_done, n + 1)
                    v.tensor_tensor(act, lin, sig, ALU.mult).then_inc(act_done, 1)
                    add_combined(n + r)

            def last_combine(g, r):
                add_combined(g * BODY + r)
                dve.wait_ge(comb_free, 2 * TT * (g * BODY + r + 1) + 2)

            def next_places():
                v.tensor_scalar(place, place, -float(CAP), None, ALU.add).then_inc(round_step, 1)

            with dve.Fori(0, TURNS) as i:
                turn(i, i, 0)
            last_combine(TURNS, 0)
            next_places()
            fullest = dve.value_load(most_i[0:1, 0:1], min_val=0, max_val=T)
            with dve.Fori(1, ROUNDS) as r:
                with dve.If(fullest > r * CAP):
                    dve.wait_ge(selgt_ps, r * NE + 1)
                    dve.wait_ge(round_step, r)
                    v.memset(selGT, 0.0).then_inc(selgt_done, 1)
                    with dve.Fori(0, TURNS) as i:
                        turn(i, r * TURNS + i, r)
                    last_combine((r + 1) * TURNS, r)
                    next_places()
                with dve.Else():
                    pass
            for tt in range(TT):
                R = ROWS[tt]
                v.tensor_tensor_reduce(outp[0:R], y[0:R, tt, :], y[0:R, tt, :], 1.0, 0.0, ALU.mult, ALU.add,
                                       ysum[0:R, tt:tt + 1]).then_inc(fin_sum, 1)
                dve.wait_ge(fin_sum, tt + 1)
            dve.wait_ge(grow_in, 16)
            dve.wait_ge(fin_std, 1)
            link(v.reciprocal(yrs, yrs))
            for tt in range(TT):
                R = ROWS[tt]
                v.scalar_tensor_tensor(y[0:R, tt, :], y[0:R, tt, :], yrs[0:R, tt:tt + 1], grow[0:R],
                                       ALU.mult, ALU.mult).then_inc(y_ready, 1)

        @block.tensor
        def _(pe):
            t = nc.tensor

            def sums(i, n):
                pe.wait_ge(sq_done, i + 1)
                for k in range(KT):
                    last = t.matmul(ps[7][:, 0:n], ones, sq[i][:, k, :], start=(k == 0), stop=(k == KT - 1))
                last.then_inc(ss_done, 1)

            def unit_ready(u):
                pe.wait_ge(ring_in[u % PRE], 16 * (u // PRE + 1))
                return slot[u % PRE]

            def project(u, c, moving, n, first_h):
                w = unit_ready(u).rearrange("p (k c) -> p k c", k=KT)
                for k in range(KT):
                    if c == 0:
                        pe.wait_ge(h_done, first_h + k + 1)
                    last = t.matmul(ps[c % 4][:, 0:n], w[:, k, (c % 2) * P:(c % 2 + 1) * P], moving[:, k, :],
                                    start=(k == 0), stop=(k == KT - 1))
                last.then_inc(proj, 1)

            def token_major(src, evacuated):
                if evacuated:
                    pe.wait_ge(tok_done, evacuated)
                for tt in range(TT):
                    R = ROWS[tt]
                    for h in range(H):
                        last = t.transpose(ps[4 + tt][0:R, h * P:(h + 1) * P], src[:, h, tt * P:tt * P + R], ident)
                    last.then_inc(tok_ps, 1)

            pe.wait_ge(consts, 1)
            sums(0, T)
            for c in range(24):
                if 4 <= c < 20:
                    pe.wait_ge(evac_a, c - 3)
                elif c >= 20:
                    pe.wait_ge(evac_v, c - 4 - 15)
                project(U_IN + c // 2, c, hT, T, 0)
                if c == 7:
                    pe.wait_ge(std_done, 1)
                    sums(1, MEM)
                if c == 21:
                    pe.wait_ge(evac_v, 4)
                    token_major(pi, 0)
            for c in range(KT):
                if c < 4:
                    pe.wait_ge(evac_v, 4 + c + 1)
                else:
                    pe.wait_ge(evac_a, 16 + c - 3)
                project(U_XK + c // 2, c, memT, MEM, KT)
                if c == 1:
                    pe.wait_ge(evac_v, 8)
                    token_major(pv, TT)
            for c in range(8):
                w, mt = unit_ready(U_XV + c // 2).rearrange("p (k c) -> p k c", k=KT), c % 2
                pe.wait_ge(evac_a, 16 + 4 + c + 1 if c < 4 else 24 + c - 3)
                for k in range(KT):
                    last = t.matmul(ps[c % 4][:, 0:256], memT[:, k, mt * P:(mt + 1) * P], w[:, k, :],
                                    start=(k == 0), stop=(k == KT - 1))
                last.then_inc(proj, 1)
            pe.wait_ge(k2_done, 1)
            token_major(k2, 2 * TT)
            pe.wait_ge(std_done, 2)
            pe.wait_ge(qk1_done, 2)
            for tt in range(2):
                for h in range(H):
                    for half in range(2):
                        q = slice(tt * P + CH * half, tt * P + CH * half + CH)
                        last = t.matmul(ps[7][CH * half:CH * half + CH, (H * tt + h) * CH:(H * tt + h + 1) * CH],
                                        k1[:, h, q], q1[:, h, q], start=True, stop=True)
            last.then_inc(sc_ps, 1)
            pe.wait_ge(tok_done, 3 * TT)
            for h in range(H):
                last = t.matmul(ps[6][0:TS, h * TS:(h + 1) * TS], k1[:, h, SEQ:T], q1[:, h, SEQ:T], start=True, stop=True)
            last.then_inc(sc_ps, 1)
            pe.wait_ge(vsplit_done, 4)
            pe.wait_ge(evac_a, 32)
            for h in range(H):
                for tt in range(2):
                    last = t.matmul(ps[h][:, tt * 256:(tt + 1) * 256], ktok[:, tt, h * P:(h + 1) * P],
                                    vsplit[:, H * tt + h, :], start=True, stop=True)
                last.then_inc(upd_ps, 1)
            pe.wait_ge(consts, 2)
            for tt in range(2):
                pe.wait_ge(vn_done, tt + 1)
                for g in range(H):
                    last = t.matmul(ps[4 + tt][:, g * P:(g + 1) * P], vn[:, tt, g * P:(g + 1) * P], gw[:, g, :],
                                    start=True, stop=True)
                last.then_inc(gm_ps, 1)
            pe.wait_ge(vn_done, 3)
            pe.wait_ge(sc_done, 3)
            for g in range(H):
                last = t.matmul(ps[6][:, P + g * TS:P + (g + 1) * TS], vn[:, 2, g * P:(g + 1) * P], gwc[:, g, :],
                                start=True, stop=True)
            last.then_inc(gm_ps, 1)
            pe.wait_ge(q2_done, 1 + H)
            pe.wait_ge(chain_done, H * NCH)
            for h in range(H):
                bank, at = ps[7 if h < 2 else 0], (h % 2) * SEQ
                for tt in range(2):
                    t.matmul(bank[:, at + tt * P:at + (tt + 1) * P], vtok[:, tt, h * P:(h + 1) * P],
                             sc_p[:, H * tt + h, :], start=True, stop=False)
                    for c in range(max(1, 2 * tt), 2 * tt + 2):
                        last = t.matmul(bank[:, at + c * CH:at + (c + 1) * CH], chain[:, h, c - 1, :],
                                        q2[:, h, c * CH:(c + 1) * CH], start=False, stop=(c == 2 * tt + 1))
                if h % 2:
                    last.then_inc(o_ps, 1)
            pe.wait_ge(st_in, 16)
            for h in range(H):
                out = ps[1][TS * h:TS * (h + 1), 0:P]
                t.matmul(out, sc_s[:, h, :], vtok[:, 2, h * P:(h + 1) * P], start=True, stop=False)
                for b in range(DECB):
                    last = t.matmul(out, q2m[:, h, b * TS:(b + 1) * TS], st[:, b, h, :], start=False, stop=(b == DECB - 1))
            last.then_inc(os_ps, 1)
            pe.wait_ge(os_done, 1)
            t.transpose(ps[2][:, 0:P], o_s, ident).then_inc(os_ps, 1)
            pe.wait_ge(osq_done, 1)
            pe.wait_ge(gm_done, TT)
            for h in range(H):
                t.matmul(ps[3 + h][:, 0:T], ones, k2[:, h, :], start=True, stop=True).then_inc(on_ps, 1)
            for h in range(H):
                pe.wait_ge(vx_done, h + 1)
                if h < 2:
                    pe.wait_ge(o_done, 3)
                else:
                    pe.wait_ge(s_done, 2 * (h - 1))
                for half in range(2):
                    t.matmul(ps[1 + half if h % 2 == 0 else 7 * (1 - half)][:, :], ktok[:, 2, h * P:(h + 1) * P],
                             vx[h % 2][:, 4 * half:4 * half + 4, :].rearrange("p b c -> p (b c)"),
                             start=True, stop=True).then_inc(su_ps, 1)
            pe.wait_ge(gm_done, TT)
            pe.wait_ge(s_done, 2 * H)
            for c in range(KT):
                if c >= 4:
                    pe.wait_ge(x_add, c - 3)
                w = unit_ready(U_OUT + c // 2).rearrange("p (k c) -> p k c", k=KT)
                for k in range(KT):
                    if c == 0 and k < H:
                        pe.wait_ge(oa_done, k + 1)
                    last = t.matmul(ps[c % 4][:, 0:T], w[:, k, (c % 2) * P:(c % 2 + 1) * P], oT[:, k, :],
                                    start=(k == 0), stop=(k == KT - 1))
                last.then_inc(proj, 1)
            sums(2, T)
            pe.wait_ge(x_add, KT)
            for n in range(4):
                mt, b = n // 2, n % 2
                for c in range(4):
                    last = t.transpose(ps[3 + n][:, c * P:(c + 1) * P], kT[:, 4 * b + c, mt * P:(mt + 1) * P], ident)
                last.then_inc(km_ps, 1)
            for c in range(KT):
                if c == 3:
                    pe.wait_ge(km_done, 1)
                if c >= 4:
                    pe.wait_ge(q_ev_v if c % 2 else q_ev_a, (c - 4) // 2 + 1)
                project(U_XQ + c // 2, c, hT, T, 2 * KT)
            pe.wait_ge(q_ev_a, KT // 2)
            pe.wait_ge(q_ev_v, KT // 2)
            pe.wait_ge(km_done, 4)
            for n in range(4):
                tt, hp = n // 2, n % 2
                for a in range(2):
                    for dc in range(2):
                        c = 2 * (2 * hp + a) + dc
                        last = t.matmul(ps[4 + n][:, a * MEM:(a + 1) * MEM], qT[:, c, tt * P:(tt + 1) * P], kT[:, c, :],
                                        start=(dc == 0), stop=(dc == 1))
                last.then_inc(p_score, 1)
            pe.wait_ge(qm_done, KT)
            for b in range(DECB):
                w = unit_ready(U_KC + b).rearrange("p (k m) -> p k m", k=KT)
                for dc in range(2):
                    for h in range(H):
                        c = 2 * h + dc
                        last = t.matmul(ps[0][TS * h:TS * (h + 1), 0:MEM], qm[:, c, b * TS:(b + 1) * TS], w[:, c, :],
                                        start=(b == 0 and dc == 0), stop=(b == DECB - 1 and dc == 1))
                last.then_inc(kv_used, 1)
            pe.wait_ge(p_done, 8)
            for k in range(4):
                mt, hp = k // 2, k % 2
                for a in range(2):
                    for tt in range(2):
                        last = t.transpose(ps[1 + k][:, a * SEQ + tt * P:a * SEQ + (tt + 1) * P],
                                           pr[:, H * tt + 2 * hp + a, mt * P:(mt + 1) * P], ident)
                last.then_inc(pt_ps, 1)
            pe.wait_ge(pt_done_a, 2)
            pe.wait_ge(pt_done_v, 2)
            pe.wait_ge(sp_done, 1)
            for mt in range(2):
                last = t.transpose(ps[1][:, mt * P:(mt + 1) * P], pr_s[:, mt * P:(mt + 1) * P], ident)
            last.then_inc(st_ps, 1)
            for c in range(KT):
                if c >= 3:
                    pe.wait_ge(pv_done_v if (c - 3) % 2 else pv_done_a, (c - 3) // 2 + 1)
                for mt in range(2):
                    last = t.matmul(ps[5 + c % 3][:, 0:SEQ], vM[:, mt, c * P:(c + 1) * P], prT[:, mt, c // 2, :],
                                    start=(mt == 0), stop=(mt == 1))
                last.then_inc(pv_ps, 1)
            pe.wait_ge(pm_done, 8)
            for b in range(DECB):
                w = unit_ready(U_VC + b).rearrange("p (m c) -> p m c", m=2)
                for mt in range(2):
                    for h in range(H):
                        last = t.matmul(ps[2][TS * h:TS * (h + 1), 0:256], pmT[:, mt, h, b * TS:(b + 1) * TS],
                                        w[:, mt, h * 256:(h + 1) * 256],
                                        start=(b == 0 and mt == 0), stop=(b == DECB - 1 and mt == 1))
                last.then_inc(kv_used, 1)
            pe.wait_ge(ox_done, 1)
            for dc in range(2):
                last = t.transpose(ps[3][:, dc * P:(dc + 1) * P], o_x[:, dc * P:(dc + 1) * P], ident)
            last.then_inc(oxT_ps, 1)
            pe.wait_ge(pv_done_a, KT // 2)
            pe.wait_ge(pv_done_v, KT // 2)
            pe.wait_ge(oxT_done, 2)
            for c in range(KT):
                if c >= 4:
                    pe.wait_ge(x_add, KT + c - 3)
                w = unit_ready(U_XO + c // 2).rearrange("p (k c) -> p k c", k=KT)
                for k in range(KT):
                    last = t.matmul(ps[c % 4][:, 0:T], w[:, k, (c % 2) * P:(c % 2 + 1) * P], oT[:, k, :],
                                    start=(k == 0), stop=(k == KT - 1))
                last.then_inc(proj, 1)
            sums(3, T)
            pe.wait_ge(x_add, 2 * KT)
            for tt in range(TT):
                R = ROWS[tt]
                for half in range(2):
                    for k in range(4):
                        last = t.transpose(ps[2 * tt + half][0:R, k * P:(k + 1) * P],
                                           xT[:, 4 * half + k, tt * P:tt * P + R], ident)
                    last.then_inc(y_ps, 1)
            pe.wait_ge(wr_in, 32)
            for k in range(KT):
                pe.wait_ge(h_done, 3 * KT + k + 1)
                last = t.matmul(ps[6][0:NE, 0:T], wr[:, k, :], hT[:, k, :], start=(k == 0), stop=(k == KT - 1))
            last.then_inc(lg_ps, 1)
            pe.wait_ge(lg_done, 1)
            for tt in range(TT):
                R = ROWS[tt]
                last = t.transpose(ps[7][0:R, tt * NE:(tt + 1) * NE], std[0:NE, tt * P:tt * P + R], ident[0:NE, 0:NE])
            last.then_inc(lt_ps, 1)
            pe.wait_ge(chosen_done, 1)
            for tt in range(TT):
                for s in range(tt + 1):
                    t.matmul(ps[6][:, tt * NE:(tt + 1) * NE], tri if s == tt else ones, chosen[:, s, :],
                             start=(s == 0), stop=(s == tt))
            for s in range(TT):
                last = t.matmul(ps[6][:, TT * NE:(TT + 1) * NE], ones, chosen[:, s, :], start=(s == 0), stop=(s == TT - 1))
            last.then_inc(pos_ps, 1)

            def gather():
                for d in range(KT):
                    for tt in range(TT):
                        for s in range(3):
                            last = t.matmul(ps[4 + d // 4][:, (d % 4) * P:(d % 4 + 1) * P],
                                            hx[:, s, tt, d * P:(d + 1) * P], sel[:, tt, :],
                                            start=(tt == 0 and s == 0), stop=(tt == TT - 1 and s == 2))
                last.then_inc(xg_ps, 1)

            pe.wait_ge(gates_done, 1)
            for tt in range(TT):
                last = t.transpose(ps[7][0:NE, tt * P:(tt + 1) * P], gates[:, tt, :], ident)
            last.then_inc(gt_ps, 1)
            pe.wait_ge(sel_done, 1)
            pe.wait_ge(h_split, 3)
            pe.wait_ge(y_ev_a, TT)
            pe.wait_ge(y_ev_v, TT)
            gather()
            pe.wait_ge(gt_done, 1)
            pe.wait_ge(b2_in, 16)
            for n in range(2 * TT):
                tt, half = n // 2, n % 2
                t.matmul(ps[[0, 1, 2, 3, 6, 7][n]][0:ROWS[tt], :], gatesT[0:NE, tt * P:tt * P + ROWS[tt]],
                         b2s[0:NE, half * 512:(half + 1) * 512], start=True, stop=True).then_inc(b2_ps, 1)

            def combine(c):
                for q in range(2 * TT):
                    tt, half = q // 2, q % 2
                    pe.wait_ge(comb_free, 2 * TT * c + q + 1)
                    t.matmul(ps[6 + half][0:ROWS[tt], :], selGT[:, tt * P:tt * P + ROWS[tt]],
                             outp[:, half * 512:(half + 1) * 512], start=True, stop=True).then_inc(comb_ps, 1)

            def turn(g, r):
                for j in range(BODY):
                    n = g * BODY + j
                    slots = xg[(j // 2) % 2][:, :, CAP * (j % 2):CAP * (j % 2) + CAP]

                    def expert_unit(u):
                        s, fill = (EXP_UNITS * j + u + PRE) % SLOTS, (EXP_UNITS * j + u) // SLOTS
                        pe.wait_ge(ring_in[s], (BODY * EXP_UNITS // SLOTS * g + (fills(s) + fill + 1)) * 16)
                        return slot[s]

                    pe.wait_ge(oh_done, n + 1)
                    pe.wait_ge(xg_done, g * BODY + 2 * (j // 2 + 1))
                    parts = [(ps[q // 2][CAP * (q % 2):CAP * (q % 2) + CAP, :], slice(512 * q, 512 * q + 512)) for q in range(4)]
                    for out, col in parts:
                        t.matmul(out, oh[j % 2][0:96], b1s[0:96, col], start=True, stop=False)
                    for k in range(KT):
                        w = expert_unit(k)
                        for out, col in parts:
                            last = t.matmul(out, slots[:, k, :], w[:, col], start=False, stop=(k == KT - 1))
                        last.then_inc(units_used, 1)
                    pe.wait_ge(outp_done, 2 * (n + 1))
                    pe.wait_ge(selgt_done, n + r + 1)
                    combine(n + r)
                    if j % 2:
                        pe.wait_ge(sel_done, g * (BODY // 2) + j // 2 + 2)
                        gather()
                    pe.wait_ge(act_done, n + 1)
                    if j % 2:
                        pe.wait_ge(xg_done, g * BODY + 2 * (j // 2 + 2))
                    for a in range(4):
                        last = t.transpose(ps[4][:, a * P:(a + 1) * P], act[:, a * P:(a + 1) * P], ident)
                    last.then_inc(actt_ps, 1)
                    pe.wait_ge(selg_done, n + 1)
                    for tt in range(TT):
                        last = t.transpose(ps[5][:, tt * P:(tt + 1) * P], selG[:, tt, :], ident)
                    last.then_inc(selgt_ps, 1)
                    pe.wait_ge(actt_done, n + 1)
                    for a in range(W2_UNITS):
                        w = expert_unit(W1_UNITS + a).rearrange("p (h c) -> p h c", h=2)
                        for ds in range(2):
                            for cg in range(2):
                                last = t.matmul(ps[2 + ds][CAP * cg:CAP * cg + CAP, :],
                                                actT[:, a * P + CAP * cg:a * P + CAP * cg + CAP],
                                                w[:, cg, 512 * ds:512 * ds + 512], start=(a == 0), stop=(a == W2_UNITS - 1))
                        last.then_inc(units_used, 1)

            def last_combine(g, r):
                pe.wait_ge(outp_done, 2 * (g * BODY + 1))
                pe.wait_ge(selgt_done, g * BODY + r + 1)
                combine(g * BODY + r)

            pe.wait_ge(b2_added, 2 * TT)
            pe.wait_ge(b1_split, 1)
            with pe.Fori(0, TURNS) as i:
                turn(i, 0)
            last_combine(TURNS, 0)
            pe.wait_ge(most_done, 1)
            fullest = pe.value_load(most_i[0:1, 0:1], min_val=0, max_val=T)
            with pe.Fori(1, ROUNDS) as r:
                with pe.If(fullest > r * CAP):
                    with pe.Fori(0, TURNS) as i:
                        turn(r * TURNS + i, r)
                    last_combine((r + 1) * TURNS, r)
                with pe.Else():
                    pass


def kernel(x_prompt, x_sample, mem_prompt, state_hgrn, cache_mem_k, cache_mem_v, norm_mix_g, w_in,
           hgrn_lb_logits, hgrn_norm_g, gmlp_ln_g, gmlp_ln_b, gmlp_w_s, gmlp_b_s, w_out, norm_x_g,
           norm_mem_g, w_xq, w_xk, w_xv, w_xo, norm_ffn_g, w_router, b_router, w1, b1, w2, b2, norm_final_g):
    import numpy as np
    import concourse.bacc as bacc
    from concourse.bass_utils import run_bass_kernel_spmd

    def per_partition(vector):
        return np.asarray(vector).reshape(-1, P).T

    xp, xs, mem = np.asarray(x_prompt)[0], np.asarray(x_sample).reshape(TS, D), np.asarray(mem_prompt)[0]
    cols = np.concatenate([per_partition(norm_mix_g), per_partition(norm_mem_g), per_partition(norm_x_g),
                           per_partition(norm_ffn_g), per_partition(hgrn_lb_logits), per_partition(hgrn_norm_g)], axis=1)
    b_s, w_s = np.asarray(gmlp_b_s)[0], np.asarray(gmlp_w_s)[0]
    bias = np.concatenate([np.tile(b_s, (1, SEQ // P)), np.tile(b_s[:, :DECL], (1, DECB))], axis=1)
    rows = np.concatenate([np.asarray(gmlp_ln_g).reshape(-1), np.asarray(gmlp_ln_b).reshape(-1), bias.reshape(-1)])
    w_st = w_s.transpose(2, 0, 1)
    k_t = np.asarray(cache_mem_k)[0].reshape(DECB, MEM, D).transpose(0, 2, 1)
    arrays = dict(
        x_t=np.concatenate([xp, xs]).T, mem_t=mem.T, cols=cols, rows=rows,
        b_router=np.asarray(b_router).reshape(NE, 1), w_router=w_router[0], w_in=w_in[0], w_xk=w_xk[0],
        w_xv=w_xv[0], w_out=w_out[0], w_xq=w_xq[0], w_xo=w_xo[0], k_t=k_t,
        v_c=np.asarray(cache_mem_v)[0].reshape(DECB, MEM, D), s0=np.asarray(state_hgrn).reshape(DECB * H, P, P),
        gw_t=w_st, gwc_t=np.tile(w_st[:DECL, :, :DECL], (DECB, 1, DECB)), ffn_g=norm_ffn_g[0],
        fin_g=norm_final_g, w1=w1[0], b1=b1[0], w2=w2[0], b2=b2[0])
    shapes = dict(y_p=[SEQ, D], y_s=[TS, D], s_p=[H, P, P], mk_p=[MEM, D], mv_p=[MEM, D], s_s=[DECB * H, P, P],
                  gv_s=[TS, H * P])
    nc = bacc.Bacc("TRN2", target_bir_lowering=False, num_devices=1)
    arrays = {name: np.ascontiguousarray(a) for name, a in arrays.items()}
    dram = {name: nc.dram_tensor(name, a.shape, mybir.dt.from_np(a.dtype), kind="ExternalInput").ap()
            for name, a in arrays.items()}
    dram.update({name: nc.dram_tensor(name, shape, F32, kind="ExternalOutput").ap() for name, shape in shapes.items()})
    hybrid_decoder_step(nc, **dram)
    out = run_bass_kernel_spmd(nc, [arrays], core_ids=[0]).results[0]
    return (out["y_p"].reshape(1, SEQ, D), out["y_s"].reshape(DECB, DECL, D), out["s_p"].reshape(1, 1, H, P, P),
            out["mk_p"].reshape(1, 1, MEM, H, MEM), out["mv_p"].reshape(1, 1, MEM, H, MEM),
            out["s_s"].reshape(1, DECB, H, P, P), out["gv_s"].reshape(1, DECB, DECL, H, P))
```

```python
from contextlib import ExitStack

import concourse.bass as bass
from concourse import mybir

F32 = mybir.dt.float32
BF16 = mybir.dt.bfloat16
I32 = mybir.dt.int32
U32 = mybir.dt.uint32
F32R = mybir.dt.float32r
ALU = mybir.AluOpType
ACT = mybir.ActivationFunctionType
AX = mybir.AxisListType.X

P = 128
D = 1024
KT = D // P
SEQ, DECB, DECL = 256, 8, 4
TS = DECB * DECL
T = SEQ + TS
TT = 3
ROWS = [128, 128, TS]
H = 4
CH = 64
NCH = SEQ // CH
MEM = 256
NE = 32
TOPK = 4
CAP = 64
ROUNDS = -(-T // CAP)
LIMIT, ALPHA, EPS = 7.0, 1.702, 1e-6
X_SCALE = (D // H) ** -0.5

SLOT = 2048
SLOTS = 16
PRE = 6
RING = SLOTS * SLOT
C_CELLS = 2200
X_AT = RING + C_CELLS
M_AT = X_AT + 2 * KT * T
CELLS = 53200
W1_UNITS, W2_UNITS = 8, 4
EXP_UNITS = W1_UNITS + W2_UNITS
BODY = 4
TURNS = NE // BODY
U_IN, U_XK, U_XV, U_OUT, U_XQ, U_KC, U_VC, U_XO = 0, 12, 16, 20, 24, 28, 36, 44
PRE_UNITS = 48
SPLIT_UNITS = [u + i for u in (U_XV, U_OUT, U_XQ, U_XO) for i in range(4)]
HELD = 5
IN_BASE = [512, 1024, 2560, 0, 1536, 2048]
C_MIX, C_MEM, C_X, C_FFN, C_LB, C_HN, C_N = 0, 8, 16, 24, 32, 40, 44
UPD_BANK = [4, 5, 6, 3]
NORM_BANK = [3, 5, 6, 7]
STATE_BANK = [[4, 3], [5, 6]]
GM_BANK = [7, 4, 3]
Y_BANK = [3, 4, 5, 7, 3, 4]
F32R_PLACES = ([(s * SLOT, SLOT) for s in range(8)] + [(8 * SLOT, KT * T)] + [(s * SLOT, SLOT) for s in range(10, 15)]
               + [(X_AT + KT * T, KT * T), (M_AT + 4096, KT * MEM),
                  (M_AT + 6144, KT * MEM), (M_AT + 8448, KT * T),
                  (M_AT + 10752, KT * T)])
R_LNG, R_LNB, R_BS, R_N = 0, 512, 1024, 1024 + H * T


def hybrid_decoder_step(nc, x_t, mem_t, cols, rows, b_router, w_router, w_in, w_xk, w_xv, w_out,
                        w_xq, w_xo, k_t, v_c, s0, gw_t, gwc_t, ffn_g, fin_g, w1, b1, w2, b2,
                        y_p, y_s, s_p, mk_p, mv_p, s_s, gv_s):
    with ExitStack() as ctx:
        with nc.sbuf_tensor("ring", [P, RING], F32) as ring, nc.sbuf_tensor("rest", [P, CELLS - RING], F32) as rest:
            pass

        def cells(at, end):
            return ring[:, at:end] if end <= RING else rest[:, at - RING:end - RING]

        places_r = {}
        place = 0
        for at, n in F32R_PLACES:
            if at > place:
                ctx.enter_context(nc.sbuf_tensor(f"below_{at}", [P, at - place], F32))
            places_r[at] = ctx.enter_context(nc.sbuf_tensor(f"split_{at}", [P, n], F32R))
            place = at + n
        ps = [ctx.enter_context(nc.psum_tensor(f"bank{i}", [P, 512], F32)) for i in range(8)]

        def sem(name):
            return ctx.enter_context(nc.semaphore(name))

        class Region:

            def __init__(self, at, end):
                self.at, self.end = at, end

            def take(self, n, *dims):
                v = cells(self.at, self.at + n)
                self.at += n
                assert self.at <= self.end, (self.at, self.end)
                if len(dims) == 2:
                    v = v.rearrange("p (a b) -> p a b", a=dims[0])
                elif len(dims) == 3:
                    v = v.rearrange("p (a b c) -> p a b c", a=dims[0], b=dims[1])
                return v

        def diagonal(v, first, skip, n_first):
            dims = [list(v.ap[0])] + ([[skip, n_first]] if n_first > 1 else []) + [[TS + DECL, DECB], [1, DECL]]
            return bass.AP(v.tensor, v.offset + first, dims)

        slot = [cells(s * SLOT, (s + 1) * SLOT) for s in range(SLOTS)]
        C = Region(RING, X_AT)
        ident, ones = C.take(P), C.take(P)
        tri, ones_b = C.take(P // 2).bitcast(BF16), C.take(P // 2).bitcast(BF16)
        iota_slot = C.take(P)
        iota_e = C.take(NE)
        pick_e = C.take(NE + 2)
        mask_c = C.take(CH)
        mask_s = C.take(TS)
        mask_q = C.take(DECB)
        vec = C.take(C_N)
        rstd, std = C.take(T), C.take(T)
        wr = C.take(KT * NE, KT, NE)
        valid = C.take(TT * NE, TT, NE)
        eps, br = C.take(1), C.take(NE)
        lbt, lb, omlb = C.take(8, 2, 4), C.take(4), C.take(4)
        lsum = C.take(4)
        logit = C.take(TT * NE, TT, NE)
        top, topi, topf = C.take(24, TT, 8), C.take(24, TT, 8), C.take(24, TT, 8)
        gate, gsum = C.take(12, TT, TOPK), C.take(3)
        chosen = C.take(TT * NE // 2).bitcast(BF16).rearrange("p (t e) -> p t e", t=TT)
        gates = C.take(TT * NE, TT, NE)
        place = C.take(TT * (NE + 2), TT, NE + 2)
        most, most_i = C.take(1), C.take(1).bitcast(I32)
        mx, nmx, psm, prn = C.take(8), C.take(8), C.take(8), C.take(8)
        smx, snm, ssm, srn = C.take(1), C.take(1), C.take(1), C.take(1)
        ysq, ysum, yrs = C.take(2 * TT, 2, TT), C.take(3), C.take(3)
        xT_at = X_AT
        xT = Region(xT_at, xT_at + KT * T).take(KT * T, KT, T)
        hT = Region(xT_at + KT * T, xT_at + 2 * KT * T).take(KT * T, KT, T)
        oT = hT
        M0 = M_AT

        def m(at, n, *dims):
            return Region(M0 + at, CELLS).take(n, *dims)

        Z = Region(PRE * SLOT, SLOTS * SLOT)
        pf, pq, pg, pu, pi, pv = (Z.take(H * T, H, T) for _ in range(6))
        vtok = Z.take(TT * 512, TT, 512)
        vsplit = Z.take(8 * 256, 8, 256)
        ktok = Z.take(TT * 512, TT, 512)
        vn = Z.take(TT * 512, TT, 512)
        row = Z.take(R_N)
        gw, gwc = Z.take(H * P, H, P), Z.take(H * TS, H, TS)
        chain = Z.take(H * NCH * P, H, NCH, P)
        bsum = Z.take(H * T, H, T)
        sc_s, o_s = Z.take(H * TS, H, TS), Z.take(P)
        reset = Z.take(T)
        dec_p, dec_s, b_mid = Z.take(16, H, NCH), Z.take(32, H, DECB), Z.take(16, H, NCH)
        bst, mv = Z.take(12 * 6, 12, 6), Z.take(12 * 2, 12, 2)
        lrs = Z.take(12)
        rstd_m = pu[:, 0, 0:MEM]
        k1, q1, k2, q2 = pf, pq, pi, pv
        vx = [cells(a, a + D).rearrange("p (b c) -> p b c", b=DECB)
              for a in (PRE * SLOT, PRE * SLOT + H * T)]
        slot_r = {s: places_r[s * SLOT][:, :] for s in range(SLOTS) if s * SLOT in places_r and s != 8}
        w_upper = [slot_r[10], slot_r[6], slot_r[7]]

        def split_tile(at):
            return places_r[at][:, :].rearrange("p (k t) -> p k t", k=KT)
        oT_upper, oT_lower = split_tile(8 * SLOT), split_tile(xT_at + KT * T)
        g_at = PRE * SLOT + 2 * H * T
        sq = [cells(g_at, g_at + KT * T).rearrange("p (k t) -> p k t", k=KT), m(0, KT * MEM, KT, MEM),
              m(6144, KT * T, KT, T)]
        hX = m(8448, KT * T, KT, T)
        memT_upper, memT_lower = (q.rearrange("p (k t) -> p k t", k=KT)
                                  for q in (places_r[M0 + 6144][:, :], places_r[M0 + 4096][:, :]))
        hX_upper, hX_lower = split_tile(M0 + 10752), split_tile(M0 + 8448)
        kT = m(0, KT * MEM, KT, MEM)
        vM = m(2048, 2 * D, 2, D)
        memT = m(4096, KT * MEM, KT, MEM)
        kM = m(4096, 2 * D, 2, D)
        ex = [m(6144, H * T, H, T), m(6144 + H * T, H * T, H, T)]
        o_raw = ex[1]
        sc_p = m(6144, 8 * P, 8, P)
        q2m = m(8448, H * 256, H, 256)
        st = m(9472, TS * P, DECB, H, P)
        st_f = m(9472, TS * P)
        qm = m(4096, KT * 256, KT, 256)
        qT = m(6144, KT * T, KT, T)
        pr = m(8448, 8 * MEM, 8, MEM)
        prT = m(10496, 8 * MEM, 2, H, MEM)
        pmT = m(6144, 8 * 256, 2, H, 256)
        pr_s, o_x = m(12544, MEM), m(12800, MEM)
        hx_f = m(0, TT * D, TT, D)
        hx = m(0, 4608).bitcast(BF16).rearrange("p (s t d) -> p s t d", s=3, t=TT)
        y = m(4608, TT * D, TT, D)
        b1f = m(8448, SLOT)
        glu, lin, sig, act = (m(7680 + 512 * i, 512) for i in range(4))
        htmp = [m(7680, D), m(8704, D), cells(xT_at + D, xT_at + 2 * D)]
        junk = m(0, 6 * 512, 2, TT, 512)
        pick_t = m(10752, TT * TOPK * NE, TT, TOPK, NE)
        actT = m(9728, 512)
        selGT = m(10240, 384)
        selG = m(10752, 384, TT, P)
        sel = m(11136, 192).bitcast(BF16).rearrange("p (t s) -> p t s", t=TT)
        oh = [m(11328 + 32 * i, 32).bitcast(BF16) for i in range(2)]
        b1s = m(11520, 1024).bitcast(BF16)
        frow = m(12544, D)
        xg = [xT_at + i * 1024 for i in range(2)]
        xg = [cells(a, a + 1024).rearrange("p (k s) -> p k s", k=KT) for a in xg]
        outp = cells(xT_at + KT * T, xT_at + KT * T + 1024)

        ring_in = [sem(f"ring_in{s}") for s in range(SLOTS)]
        units_used = sem("units_used")
        kv_used = sem("kv_used")
        x_in = [sem("x_in0"), sem("x_in1")]
        vec_in, mem_in, row_in, gw_in, st_in, wr_in, b1_in, b2_in, frow_in, grow_in = map(
            sem, "vec_in mem_in row_in gw_in st_in wr_in b1_in b2_in frow_in grow_in".split())
        mv_out, sp_out, gv_out, ss_out, mk_out, y_out = map(
            sem, "mv_out sp_out gv_out ss_out mk_out y_out".split())
        consts, lb_in, lb_exp, sq_done, sq_sum, ss_done, std_done, h_done = map(
            sem, "consts lb_in lb_exp sq_done sq_sum ss_done std_done h_done".split())
        proj, evac_a, evac_v, x_add = map(sem, "proj evac_a evac_v x_add".split())
        w_upper_done, w_split, o_split, mem_split = map(sem, "w_upper_done w_split o_split mem_split".split())
        tok_ps, tok_done, fg_done, ln_done, scan_done, ex_in, ex_done, q2_done, k2_done, qk1_done = map(
            sem, "tok_ps tok_done fg_done ln_done scan_done ex_in ex_done q2_done k2_done qk1_done".split())
        vsplit_done, sc_ps, sc_done, upd_ps, chain_done, o_ps, o_done, os_ps, os_done = map(
            sem, "vsplit_done sc_ps sc_done upd_ps chain_done o_ps o_done os_ps os_done".split())
        osq_done, on_ps, on_std, oa_done, vx_done, su_ps, s_scaled, s_done = map(
            sem, "osq_done on_ps on_std oa_done vx_done su_ps s_scaled s_done".split())
        bn_done, bn_std, vn_done, gm_ps, gm_done = map(sem, "bn_done bn_std vn_done gm_ps gm_done".split())
        km_ps, km_done, q_ev, qm_zero, qm_done = map(
            sem, "km_ps km_done q_ev qm_zero qm_done".split())
        p_score, p_max, p_exp, p_done, s_max, s_exp, sp_done = map(
            sem, "p_score p_max p_exp p_done s_max s_exp sp_done".split())
        pt_ps, pt_done_a, pt_done_v, pv_ps, pv_done_a, pv_done_v = map(
            sem, "pt_ps pt_done_a pt_done_v pv_ps pv_done_a pv_done_v".split())
        st_ps, pm_zero, pm_done, ox_done, oxT_ps, oxT_done = map(
            sem, "st_ps pm_zero pm_done ox_done oxT_ps oxT_done".split())
        y_ps, y_sq, y_ev, y_sum, lg_ps, lg_done, lt_ps, gate_in, gate_exp, chosen_done, gates_done = map(
            sem, "y_ps y_sq y_ev y_sum lg_ps lg_done lt_ps gate_in gate_exp chosen_done gates_done".split())
        pos_ps, logit_done, gt_ps, most_done, b1_split, y_std, h_tok, h_hi, h_rest, h_mid, h_split = map(
            sem, "pos_ps logit_done gt_ps most_done b1_split y_std h_tok h_hi h_rest h_mid h_split".split())
        oh_done, sel_done, selg_done, selgt_ps, selgt_done, xg_ps, xg_done = map(
            sem, "oh_done sel_done selg_done selgt_ps selgt_done xg_ps xg_done".split())
        glu_done, lin_done, sig_done, prod_done, act_done, actt_ps, actt_done, outp_done, comb_ps, comb_free = map(
            sem, "glu_done lin_done sig_done prod_done act_done actt_ps actt_done outp_done comb_ps comb_free".split())
        hx_zero, selgt_zero, rounds_done, fin_sum, fin_std, y_ready, round_step = map(
            sem, "hx_zero selgt_zero rounds_done fin_sum fin_std y_ready round_step".split())
        dve_step, act_step, pool_step = map(sem, "dve_step act_step pool_step".split())

        block = ctx.enter_context(nc.Block())

        def unit_src(u):
            def square(w, c):
                return w[:, c:c + 256].rearrange("(k p) c -> p k c", p=P)
            if u < U_XK:
                return square(w_in, IN_BASE[u // 2] + 256 * (u % 2))
            if u >= U_XO:
                return square(w_xo, 256 * (u - U_XO))
            if u >= U_VC:
                return v_c[u - U_VC].rearrange("(k p) c -> p k c", p=P)
            if u >= U_KC:
                return k_t[u - U_KC].rearrange("(k p) c -> p k c", p=P)
            w, first = [(w_xk, U_XK), (w_xv, U_XV), (w_out, U_OUT), (w_xq, U_XQ)][(u - U_XK) // 4]
            return square(w, 256 * (u - first))

        def load_expert_unit(eng, e, j):
            s, q = (j + PRE) % SLOTS, j % EXP_UNITS
            e = e + j // EXP_UNITS
            if q < W1_UNITS:
                return eng.dma_start(slot[s], w1[e, q * P:(q + 1) * P, :]).then_inc(ring_in[s], 16)
            q -= W1_UNITS
            return eng.dma_start(slot[s].rearrange("p (h c) -> p h c", h=2),
                                 w2[e, :, :].rearrange("(h j p) c -> j p h c", h=2, p=P)[q]).then_inc(ring_in[s], 16)

        def wait_unit_used(eng, u):
            if U_KC <= u < U_XO:
                eng.wait_ge(kv_used, u - U_KC + 1)
            else:
                eng.wait_ge(proj, 2 * (u if u < U_KC else u - (U_XO - U_KC)) + 2)

        def unit_slot(u):
            return u % PRE if u < U_XO else PRE + HELD + u - U_XO

        def unit_fill(u):
            return u // PRE + 1 if u < U_XO else 1

        def fills(s):
            return sum(unit_slot(u) == s for u in range(PRE_UNITS))

        def further_rounds(eng, fullest, one_round):
            with eng.If(fullest > CAP):
                one_round(1)
                with eng.Fori(2, ROUNDS) as r:
                    with eng.If(fullest > r * CAP):
                        one_round(r)
                    with eng.Else():
                        pass
            with eng.Else():
                pass

        @block.sync
        def _(sp):
            for a in range(2):
                sp.dma_start(xT[:, 4 * a:4 * a + 4, :],
                             x_t[512 * a:512 * a + 512, :].rearrange("(k p) t -> p k t", p=P)).then_inc(x_in[a], 16)
            def load_unit(u):
                src = unit_src(u)
                sp.dma_start(slot[unit_slot(u)].rearrange("p (k c) -> p k c", k=src.shape[1]), src
                             ).then_inc(ring_in[unit_slot(u)], 16)

            for u in range(U_XO):
                if u >= PRE:
                    wait_unit_used(sp, u - PRE)
                load_unit(u)
                if u == U_OUT + PRE:
                    sp.wait_ge(s_done, 2 * H)
                    sp.wait_ge(gm_done, TT)
                    sp.wait_ge(sp_out, 16)
                    sp.wait_ge(gv_out, 16)
                if U_OUT + PRE <= u < U_OUT + PRE + 4:
                    load_unit(U_XO + u - U_OUT - PRE)
                if u == U_OUT + PRE + 4:
                    for j in range(HELD + 4, SLOTS - PRE):
                        load_expert_unit(sp, 0, j)

            def turn(i, g, first=0):
                for j in range(first, BODY * EXP_UNITS):
                    sp.wait_ge(units_used, g * (BODY * EXP_UNITS) + j - SLOTS + 1)
                    load_expert_unit(sp, i * BODY, j)

            for u in range(U_XO - PRE, U_XO):
                wait_unit_used(sp, u)
                load_expert_unit(sp, 0, SLOTS - PRE + u % PRE)
            for j, u in enumerate((U_XO + 1, U_XO + 2) + (U_XO + 3,) * (HELD + 2)):
                wait_unit_used(sp, u)
                load_expert_unit(sp, 0, j)
            turn(0, 0, first=SLOTS)
            with sp.Fori(1, TURNS) as i:
                turn(i, i)
            sp.wait_ge(most_done, 1)
            fullest = sp.value_load(most_i[0:1, 0:1], min_val=0, max_val=T)

            def one_round(r):
                with sp.Fori(0, TURNS) as i:
                    turn(i, r * TURNS + i)
            further_rounds(sp, fullest, one_round)
            for tt in range(TT):
                sp.wait_ge(y_ready, tt + 1)
                dst = y_p[tt * P:(tt + 1) * P, :] if tt < 2 else y_s
                sp.dma_start(dst, y[0:ROWS[tt], tt, :]).then_inc(y_out, 16)
            for stored, n in ((mv_out, 1), (sp_out, 1), (gv_out, 1), (ss_out, 1), (mk_out, 2), (y_out, TT)):
                sp.wait_ge(stored, 16 * n)

        @block.gpsimd
        def _(pool):
            steps = [0]

            def link(ins):
                steps[0] += 1
                ins.then_inc(pool_step, 1)
                pool.wait_ge(pool_step, steps[0])

            link(pool.memset(eps, EPS))
            link(pool.memset(ones, 1.0))
            link(pool.memset(ident, 0.0))
            link(pool.affine_select(out=ident, in_=ident, compare_op=ALU.not_equal, fill=1.0, base=0,
                                    pattern=[[-1, P]], channel_multiplier=1))
            link(pool.memset(ysq, 1.0))
            link(pool.memset(reset, 1.0))
            link(pool.memset(reset[:, 0:SEQ:CH], 0.0))
            pool.memset(reset[:, SEQ:T:DECL], 0.0).then_inc(consts, 1)
            pool.dma_start(memT, mem_t.rearrange("(k p) t -> p k t", p=P)).then_inc(mem_in, 16)
            pool.dma_start(row, rows.partition_broadcast(P)).then_inc(row_in, 16)
            link(pool.memset(gwc, 0.0))
            pool.dma_start(gw, gw_t).then_inc(gw_in, 16)
            pool.dma_start(gwc[0:TS], gwc_t).then_inc(gw_in, 16)
            def add_squares(i):
                pool.wait_ge(sq_done, i + 1)
                for n in (4, 2):
                    link(pool.tensor_tensor(sq[i][:, 0:n, :], sq[i][:, 0:n, :], sq[i][:, n:2 * n, :], ALU.add))
                pool.tensor_tensor(sq[i][:, 0, :], sq[i][:, 0, :], sq[i][:, 1, :], ALU.add).then_inc(sq_sum, 1)

            add_squares(0)
            link(pool.memset(vtok[:, 2, :], 0.0))
            link(pool.memset(ktok[:, 2, :], 0.0))
            link(pool.memset(vn[:, 2, :], 0.0))
            link(pool.memset(vsplit, 0.0))
            link(pool.memset(mv, 1.0))
            pool.memset(q2m, 0.0).then_inc(consts, 1)
            pool.dma_start(st_f.rearrange("p (b v) -> p b v", v=P), s0.rearrange("n k v -> k n v")).then_inc(st_in, 16)
            pool.dma_start(wr, w_router.rearrange("(k p) e -> p k e", p=P)).then_inc(wr_in, 16)
            pool.dma_start(br, b_router.partition_broadcast(P)).then_inc(wr_in, 16)
            link(pool.memset(ones_b, 1.0))
            link(pool.memset(tri, 1.0))
            link(pool.affine_select(out=tri, in_=tri, compare_op=ALU.is_gt, fill=0.0, base=0,
                                    pattern=[[1, P]], channel_multiplier=-1))
            link(pool.iota(iota_slot.rearrange("p (a b) -> p a b", a=2), pattern=[[0, 2], [1, CAP]], base=0,
                           channel_multiplier=0, allow_small_or_imprecise_dtypes=True))
            link(pool.iota(iota_e, pattern=[[1, NE]], base=0, channel_multiplier=0,
                           allow_small_or_imprecise_dtypes=True))
            link(pool.memset(pick_e, 0.0))
            for a in range(3):
                q = pick_e[32 * a:32 * a + 32]
                link(pool.affine_select(out=q, in_=q, compare_op=ALU.not_equal, fill=1.0, base=0,
                                        pattern=[[-1, NE + 2]], channel_multiplier=1))
                link(pool.affine_select(out=q, in_=q, compare_op=ALU.not_equal, fill=1.0, base=NE,
                                        pattern=[[-1, NE + 2]], channel_multiplier=1))
            link(pool.memset(mask_c, 1.0))
            for a in range(2):
                q = mask_c[CH * a:CH * a + CH]
                link(pool.affine_select(out=q, in_=q, compare_op=ALU.is_ge, fill=0.0, base=0,
                                        pattern=[[1, CH]], channel_multiplier=-1))

            def block_causal(v, groups):
                g = [[0, groups]] if groups > 1 else []
                for pattern, mult in (([[-DECL, DECB], [0, DECL]], 1), ([[DECL, DECB], [1, DECL]], -1)):
                    link(pool.affine_select(out=v, in_=v, compare_op=ALU.is_ge, fill=0.0, base=0,
                                            pattern=g + pattern, channel_multiplier=mult))

            link(pool.memset(mask_s, 1.0))
            block_causal(mask_s.rearrange("p (b t) -> p b t", b=DECB), 1)
            link(pool.memset(mask_q, 1.0))
            for base, step, mult in ((0, -DECL, 1), (DECL - 1, DECL, -1)):
                link(pool.affine_select(out=mask_q, in_=mask_q, compare_op=ALU.is_ge, fill=0.0, base=base,
                                        pattern=[[step, DECB]], channel_multiplier=mult))
            link(pool.memset(valid, 1.0))
            link(pool.affine_select(out=valid[:, 2, :], in_=valid[:, 2, :], compare_op=ALU.is_ge, fill=0.0,
                                    base=TS - 1, pattern=[[0, NE]], channel_multiplier=-1))
            link(pool.memset(logit, 0.0))
            link(pool.memset(sc_s, 0.0))
            pool.wait_ge(gw_in, 32)
            link(pool.affine_select(out=gw, in_=gw, compare_op=ALU.is_ge, fill=0.0, base=0,
                                    pattern=[[0, H], [1, P]], channel_multiplier=-1))
            block_causal(gwc.rearrange("p g (b t) -> p g b t", b=DECB), H)
            pool.wait_ge(wr_in, 32)
            pool.wait_ge(vec_in, 16)
            pool.tensor_tensor(wr, wr, vec[:, C_FFN:C_FFN + KT].unsqueeze(2).to_broadcast([P, KT, NE]),
                               ALU.mult).then_inc(consts, 1)

            add_squares(1)

            def lower_part(i):
                u = slot[unit_slot(SPLIT_UNITS[i])]
                pool.wait_ge(w_upper_done, i + 1)
                pool.tensor_tensor(slot_r[unit_slot(SPLIT_UNITS[i])], u, w_upper[i % 3], ALU.subtract).then_inc(w_split, 1)

            pool.wait_ge(ex_done, 2)
            pool.wait_ge(st_in, 16)
            pool.wait_ge(os_ps, 1)
            for h in range(H):
                pool.tensor_tensor(st[:, :, h, :], st[:, :, h, :],
                                   dec_s[:, h, :].unsqueeze(2).to_broadcast([P, DECB, P]),
                                   ALU.mult).then_inc(s_scaled, 1)
            for i in range(7):
                lower_part(i)
            pool.wait_ge(sq_done, 3)
            for k in range(1, KT):
                pool.wait_ge(sq_done, 2 + k + 1)
                if k > 1:
                    pool.wait_ge(sq_sum, 2 + k - 1)
                pool.tensor_tensor(sq[2][:, 0, :], sq[2][:, 0, :], sq[2][:, k, :], ALU.add).then_inc(sq_sum, 1)
                if k % 2:
                    lower_part(7 + k // 2)
            lower_part(11)
            pool.wait_ge(mk_out, 32)
            pool.memset(qm, 0.0).then_inc(qm_zero, 1)
            for i in (12, 13, 14):
                lower_part(i)
            pool.wait_ge(kv_used, DECB)
            pool.memset(pmT, 0.0).then_inc(pm_zero, 1)

            pool.wait_ge(pt_ps, 4)
            for k in range(3):
                pool.dma_start(b1f[32 * k:32 * k + 32], b1).then_inc(b1_in, 16)
            pool.wait_ge(oxT_ps, 1)
            pool.dma_start(frow, ffn_g.partition_broadcast(P)).then_inc(frow_in, 16)
            lower_part(15)
            pool.wait_ge(y_sq, 2 * TT)
            pool.memset(hx[:, :, 2, :], 0.0).then_inc(hx_zero, 1)

            for tt in range(TT):
                R = ROWS[tt]
                pool.wait_ge(h_hi, tt + 1)
                pool.tensor_tensor(htmp[tt][0:R], htmp[tt][0:R], hx[0:R, 0, tt, :], ALU.subtract).then_inc(h_rest, 1)
            pool.wait_ge(outp_done, 2)
            pool.dma_start(outp[0:NE], b2).then_inc(b2_in, 16)
            pool.wait_ge(h_tok, TT)
            pool.dma_start(frow, fin_g.partition_broadcast(P)).then_inc(grow_in, 16)

        @block.scalar
        def _(act_e):
            a = nc.scalar

            a.dma_start(vec, cols).then_inc(vec_in, 16)

            def squares(i, src):
                a.activation(sq[i], src, ACT.Square).then_inc(sq_done, 1)

            def root(i, n):
                act_e.wait_ge(ss_done, i + 1)
                a.activation(std[:, 0:n], ps[7][:, 0:n], ACT.Sqrt, bias=eps, scale=1.0 / D).then_inc(std_done, 1)

            act_e.wait_ge(x_in[0], 16)
            act_e.wait_ge(x_in[1], 16)
            squares(0, xT)
            act_e.wait_ge(lb_in, 1)
            a.activation(lbt, lbt, ACT.Exp).then_inc(lb_exp, 1)
            act_e.wait_ge(consts, 1)
            root(0, T)

            def through(dst, fn, first):
                for h in range(H):
                    act_e.wait_ge(evac_v, first + h + 1)
                    a.activation(dst[:, h, :], dst[:, h, :], fn).then_inc(evac_a, 1)

            through(pf, ACT.Sigmoid, 0)
            act_e.wait_ge(mem_in, 16)
            squares(1, memT)
            act_e.wait_ge(fg_done, H)
            a.activation(ex[0], pf, ACT.Ln).then_inc(ln_done, 1)
            act_e.wait_ge(scan_done, H)
            a.activation(dec_p, bsum[:, :, CH - 1:SEQ:CH], ACT.Exp).then_inc(ex_done, 1)
            a.activation(dec_s, bsum[:, :, SEQ + DECL - 1:T:DECL], ACT.Exp).then_inc(ex_done, 1)
            act_e.wait_ge(ex_in, 1)
            a.activation(ex[0], ex[0], ACT.Exp).then_inc(ex_done, 1)
            act_e.wait_ge(consts, 2)
            for tt in range(TT):
                act_e.wait_ge(tok_ps, tt + 1)
                a.copy(vtok[0:ROWS[tt], tt, :], ps[4 + tt][0:ROWS[tt], :]).then_inc(tok_done, 1)
            root(1, MEM)
            a.activation(ex[1], bsum, ACT.Exp).then_inc(ex_done, 1)
            for tt in range(TT):
                act_e.wait_ge(tok_ps, TT + tt + 1)
                a.activation(vn[0:ROWS[tt], tt, :], ps[4 + tt][0:ROWS[tt], :], ACT.Gelu_apprx_tanh).then_inc(tok_done, 1)
            through(pq, ACT.Silu, 12)
            act_e.wait_ge(ex_in, 2)
            a.activation(ex[1], bsum, ACT.Exp).then_inc(ex_done, 1)
            a.activation(ex[0], bsum, ACT.Exp, scale=-1.0).then_inc(ex_done, 1)
            act_e.wait_ge(bn_done, 1)
            a.activation(lrs, mv[:, :, 1], ACT.Sqrt, bias=eps).then_inc(bn_std, 1)
            for tt in range(TT):
                act_e.wait_ge(tok_ps, 2 * TT + tt + 1)
                a.copy(ktok[0:ROWS[tt], tt, :], ps[4 + tt][0:ROWS[tt], :]).then_inc(tok_done, 1)
            through(pg, ACT.Silu, 16)
            for k in range(2):
                act_e.wait_ge(o_ps, k + 1)
                a.copy(o_raw[:, 2 * k:2 * k + 2, 0:SEQ],
                       ps[7 if k == 0 else 4][:, :].rearrange("p (h t) -> p h t", h=2)).then_inc(o_done, 1)
            act_e.wait_ge(os_ps, 1)
            a.copy(o_s, ps[5][:, 0:P]).then_inc(os_done, 1)
            act_e.wait_ge(os_ps, 2)
            a.copy(o_raw[:, :, SEQ:T], ps[6][:, 0:P].rearrange("p (h t) -> p h t", h=H)).then_inc(o_done, 1)
            act_e.wait_ge(o_done, 3)
            a.activation(k2, o_raw, ACT.Square).then_inc(osq_done, 1)
            for h in range(H):
                act_e.wait_ge(on_ps, h + 1)
                a.activation(bsum[:, h, :], ps[NORM_BANK[h]][:, 0:T], ACT.Sqrt, bias=eps,
                             scale=1.0 / P).then_inc(on_std, 1)
            through(pu, ACT.Gelu_apprx_tanh, 20)
            act_e.wait_ge(chain_done, H * NCH)
            a.dma_start(s_p.rearrange("h k v -> k h v"), chain[:, :, NCH - 1, :]).then_inc(sp_out, 16)
            act_e.wait_ge(vn_done, TT)
            a.dma_start(gv_s, vn[0:TS, 2, :]).then_inc(gv_out, 16)
            for c in range(KT):
                act_e.wait_ge(proj, 24 + c + 1)
                a.copy(kT[:, c, :], ps[c % 3][:, 0:MEM]).then_inc(evac_a, 1)
            for p in range(8):
                act_e.wait_ge(proj, 32 + p + 1)
                w, mt = p // 2, p % 2
                a.copy(vM[:, mt, w * 256:(w + 1) * 256], ps[(32 + p) % 3][:, 0:256]).then_inc(evac_a, 1)
                if p == 0:
                    act_e.wait_ge(s_done, 2 * H)
                    a.dma_start(s_s.rearrange("b k v -> k b v"),
                                st_f.rearrange("p (b v) -> p b v", v=P)).then_inc(ss_out, 16)
            act_e.wait_ge(evac_a, 16 + 8 + 8)
            a.dma_start(mv_p.rearrange("(m p) d -> p m d", p=P), vM).then_inc(mv_out, 16)

            for k in range(KT):
                act_e.wait_ge(x_add, k + 1)
                a.activation(sq[2][:, k, :], xT[:, k, :], ACT.Square).then_inc(sq_done, 1)
            root(2, T)
            for n in range(4):
                mt, b = n // 2, n % 2
                act_e.wait_ge(km_ps, n + 1)
                a.copy(kM[:, mt, b * 512:(b + 1) * 512], ps[3 + n][:, :]).then_inc(km_done, 1)
            act_e.wait_ge(km_done, 4)
            for mt in range(2):
                a.dma_start(mk_p[mt * P:(mt + 1) * P, :], kM[:, mt, :]).then_inc(mk_out, 16)
            act_e.wait_ge(ss_out, 16)
            for n in range(8):
                tt, h = n // 4, n % 4
                act_e.wait_ge(p_max, n // 2 + 1)
                a.activation(pr[:, n, :], ps[3 + n // 2][:, (h % 2) * MEM:(h % 2 + 1) * MEM], ACT.Exp,
                             bias=nmx[:, n:n + 1], scale=X_SCALE, accum_out=psm[:, n:n + 1]).then_inc(p_exp, 1)
            act_e.wait_ge(s_max, 1)
            a.activation(pr_s, ps[7][:, 0:MEM], ACT.Exp, bias=snm, scale=X_SCALE, accum_out=ssm).then_inc(s_exp, 1)
            for k in range(2):
                act_e.wait_ge(pt_ps, k + 1)
                a.copy(prT[:, 0, 2 * k:2 * k + 2, :], ps[3 + k][:, :].rearrange("p (h t) -> p h t", h=2)).then_inc(pt_done_a, 1)
            for c in range(0, KT, 2):
                act_e.wait_ge(pv_ps, c + 1)
                a.copy(oT[:, c, 0:SEQ], ps[c % 3][:, 0:SEQ]).then_inc(pv_done_a, 1)
            act_e.wait_ge(kv_used, 2 * DECB)
            a.copy(o_x, ps[4][:, 0:MEM]).then_inc(ox_done, 1)

            a.activation(srn, eps, ACT.Sqrt).then_inc(act_step, 1)
            for n in range(2 * TT):
                half, tt = n // TT, n % TT
                R = ROWS[tt]
                act_e.wait_ge(y_ev, n + 1)
                a.activation(junk[0:R, half, tt, :], y[0:R, tt, 512 * half:512 * half + 512], ACT.Square,
                             accum_out=ysq[0:R, half, tt:tt + 1]).then_inc(y_sq, 1)
            act_e.wait_ge(act_step, 1)
            act_e.wait_ge(y_sum, 1)
            a.activation(yrs, ysum, ACT.Sqrt, bias=eps, scale=1.0 / D).then_inc(y_std, 1)
            act_e.wait_ge(y_sq, 2 * TT)

            def middle_part(tt):
                act_e.wait_ge(h_rest, tt + 1)
                a.copy(hx[0:ROWS[tt], 1, tt, :], htmp[tt][0:ROWS[tt]]).then_inc(h_mid, 1)
            for tt in range(TT):
                act_e.wait_ge(h_tok, tt + 1)
                act_e.wait_ge(hx_zero, 1)
                a.copy(hx[0:ROWS[tt], 0, tt, :], htmp[tt][0:ROWS[tt]]).then_inc(h_hi, 1)
            for tt in range(TT):
                middle_part(tt)
            act_e.wait_ge(gate_in, 1)
            a.activation(gate, gate, ACT.Exp).then_inc(gate_exp, 1)

            def evac_gather(nth, parity):
                q = xg[parity].rearrange("p k s -> p (k s)")
                act_e.wait_ge(xg_ps, 2 * nth - 1)
                a.copy(q[:, 0:512], ps[4][:, :]).then_inc(xg_done, 1)
                act_e.wait_ge(xg_ps, 2 * nth)
                a.copy(q[:, 512:1024], ps[5][:, :]).then_inc(xg_done, 1)

            evac_gather(1, 0)
            act_e.wait_ge(gt_ps, 1)
            act_e.wait_ge(selgt_zero, 1)
            a.copy(selGT[0:NE], ps[7][0:NE, 0:384]).then_inc(selgt_done, 1)

            def turn(g):
                for j in range(BODY):
                    n = g * BODY + j
                    act_e.wait_ge(glu_done, n + 1)
                    a.activation(sig, glu, ACT.Sigmoid, scale=ALPHA).then_inc(sig_done, 1)
                    if j % 2 == 0:
                        evac_gather(g * (BODY // 2) + j // 2 + 2, (j // 2 + 1) % 2)
                    act_e.wait_ge(actt_ps, n + 1)
                    a.copy(actT, ps[4][:, :]).then_inc(actt_done, 1)
                    act_e.wait_ge(selgt_ps, n + 2)
                    a.copy(selGT, ps[5][:, 0:384]).then_inc(selgt_done, 1)
                    act_e.wait_ge(units_used, (n + 1) * EXP_UNITS)
                    a.copy(outp[:, 0:512], ps[2][:, :]).then_inc(outp_done, 1)
                    a.copy(outp[:, 512:1024], ps[3][:, :]).then_inc(outp_done, 1)

            with act_e.Fori(0, TURNS) as i:
                turn(i)
            act_e.wait_ge(most_done, 1)
            fullest = act_e.value_load(most_i[0:1, 0:1], min_val=0, max_val=T)

            def one_round(r):
                with act_e.Fori(0, TURNS) as i:
                    turn(r * TURNS + i)
            further_rounds(act_e, fullest, one_round)
            a.activation(srn, eps, ACT.Sqrt).then_inc(act_step, 1)
            act_e.wait_ge(rounds_done, 1)
            for tt in range(TT):
                R = ROWS[tt]
                a.activation(hx_f[0:R, tt, :], y[0:R, tt, :], ACT.Square, accum_out=ysum[0:R, tt:tt + 1]).then_inc(fin_sum, 1)
                act_e.wait_ge(fin_sum, tt + 1)
                a.activation(yrs[0:R, tt:tt + 1], ysum[0:R, tt:tt + 1], ACT.Sqrt, bias=eps[0:R], scale=1.0 / D).then_inc(fin_std, 1)

        @block.vector
        def _(dve):
            v = nc.vector
            steps = [0]

            def link(ins):
                steps[0] += 1
                ins.then_inc(dve_step, 1)
                dve.wait_ge(dve_step, steps[0])

            dve.wait_ge(vec_in, 16)

            def gain(c, src, dst, k):
                v.tensor_scalar(dst[:, k, :], src[:, k, :], vec[:, c + k:c + k + 1], None, ALU.mult).then_inc(h_done, 1)
            for k in range(KT):
                dve.wait_ge(x_in[k // 4], 16)
                gain(C_MIX, xT, hT, k)
            lg = vec[:, C_LB:C_LB + 8].rearrange("p (a b) -> p a b", a=2)
            link(v.tensor_tensor(lb, lg[:, 0, :], lg[:, 1, :], ALU.max))
            v.tensor_tensor(lbt, lg, lb.unsqueeze(1).to_broadcast([P, 2, H]), ALU.subtract).then_inc(lb_in, 1)
            dve.wait_ge(lb_exp, 1)
            link(v.tensor_tensor(lsum, lbt[:, 0, :], lbt[:, 1, :], ALU.add))
            link(v.reciprocal(lsum, lsum))
            link(v.tensor_tensor(lb, lbt[:, 0, :], lsum, ALU.mult))
            link(v.tensor_scalar(omlb, lb, -1.0, 1.0, ALU.mult, ALU.add))
            dve.wait_ge(std_done, 1)
            link(v.reciprocal(rstd, std))

            w_in_out = [pf, pi, pv, pq, pg, pu]

            def evac(*chunks):
                for c in chunks:
                    dve.wait_ge(proj, c + 1)
                    v.tensor_tensor(w_in_out[c // 4][:, c % 4, :], ps[c % 3][:, 0:T], rstd, ALU.mult).then_inc(evac_v, 1)

            def parts(t3):
                return (t3[:, :, 0:SEQ].rearrange("p h (c t) -> p h c t", c=NCH),
                        t3[:, :, SEQ:T].rearrange("p h (b t) -> p h b t", b=DECB))
            (bp, bs), (ep, es) = parts(bsum), parts(ex[0])

            evac(0, 1, 2, 3)
            for h in range(H):
                dve.wait_ge(evac_a, h + 1)
                v.tensor_scalar(pf[:, h, :], pf[:, h, :], omlb[:, h:h + 1], lb[:, h:h + 1],
                                ALU.mult, ALU.add).then_inc(fg_done, 1)
            evac(4, 5)
            dve.wait_ge(ln_done, 1)
            dve.wait_ge(consts, 1)
            for h in range(H):
                v.tensor_tensor_scan(bsum[:, h, :], reset, ex[0][:, h, :], 0.0, ALU.mult, ALU.add).then_inc(scan_done, 1)
            evac(6)
            link(v.tensor_scalar(pf, pf, -1.0, 1.0, ALU.mult, ALU.add))
            dve.wait_ge(scan_done, H)
            v.tensor_tensor(ep, bp[:, :, :, CH - 1:CH].to_broadcast([P, H, NCH, CH]), bp, ALU.subtract)
            v.tensor_tensor(es, bs[:, :, :, DECL - 1:DECL].to_broadcast([P, H, DECB, DECL]), bs,
                            ALU.subtract).then_inc(ex_in, 1)
            evac(7, 8)
            dve.wait_ge(tok_done, TT)
            dve.wait_ge(consts, 2)
            for tt in range(2):
                for half in range(2):
                    q = slice(CH * half, CH * half + CH)
                    v.tensor_copy(vsplit[q, 4 * tt:4 * tt + 4, P * half:P * half + P],
                                  vtok[q, tt, :].rearrange("p (h c) -> p h c", h=H)).then_inc(vsplit_done, 1)
            evac(9)
            dve.wait_ge(ex_done, 3)
            v.tensor_tensor(k2, pf, ex[0], ALU.mult).then_inc(k2_done, 1)
            evac(10)
            dve.wait_ge(std_done, 2)
            link(v.reciprocal(rstd_m, std[:, 0:MEM]))
            for k in range(KT):
                if k == 4:
                    evac(11)
                v.scalar_tensor_tensor(memT[:, k, :], memT[:, k, :], vec[:, C_MEM + k:C_MEM + k + 1], rstd_m,
                                       ALU.mult, ALU.mult).then_inc(h_done, 1)
            evac(12)
            dve.wait_ge(tok_done, 2 * TT)
            for n in range(4 * TT):
                tt, g = n // 4, n % 4
                last = v.bn_stats(bst[0:ROWS[tt], n, :], vn[0:ROWS[tt], tt, g * P:(g + 1) * P])
            link(last)
            evac(13)
            for n in range(4 * TT):
                R = ROWS[n // 4]
                last = v.bn_aggr(mv[0:R, n, :], bst[0:R, n, :])
            last.then_inc(bn_done, 1)
            evac(14, 15)
            dve.wait_ge(evac_a, 2 * H)
            dve.wait_ge(ex_done, 4)
            v.tensor_tensor(q2, pq, ex[1], ALU.mult).then_inc(q2_done, 1)
            link(v.tensor_copy(b_mid, bsum[:, :, CH // 2 - 1:SEQ:CH]))
            v.tensor_tensor(bp, bp, b_mid.unsqueeze(3).to_broadcast([P, H, NCH, CH]), ALU.subtract).then_inc(ex_in, 1)
            dve.wait_ge(q2_done, 1)
            for h in range(H):
                v.tensor_copy(diagonal(q2m, 256 * h, 0, 1),
                              q2[:, h, SEQ:T].rearrange("p (b t) -> p b t", b=DECB)).then_inc(q2_done, 1)
            evac(16)
            dve.wait_ge(ex_done, 5)
            v.tensor_tensor(q1, pq, ex[1], ALU.mult).then_inc(qk1_done, 1)
            dve.wait_ge(ex_done, 6)
            v.tensor_tensor(k1, pf, ex[0], ALU.mult).then_inc(qk1_done, 1)
            evac(17)
            dve.wait_ge(qk1_done, 2)
            link(v.memset(sc_p, 0.0))
            dve.wait_ge(bn_std, 1)
            link(v.reciprocal(lrs, lrs))
            for n in range(4 * TT):
                tt, g, R = n // 4, n % 4, ROWS[n // 4]
                q = vn[0:R, tt, g * P:(g + 1) * P]
                last = v.tensor_scalar(q, q, mv[0:R, n, 0:1], lrs[0:R, n:n + 1], ALU.subtract, ALU.mult)
            link(last)
            evac(18)
            dve.wait_ge(consts, 3)
            dve.wait_ge(sc_ps, 1)
            for half in range(2):
                q = slice(CH * half, CH * half + CH)
                v.tensor_tensor(sc_p[q, :, CH * half:CH * half + CH],
                                ps[7][q, :].rearrange("p (n t) -> p n t", t=CH),
                                mask_c[q].unsqueeze(1).to_broadcast([CH, 8, CH]), ALU.mult).then_inc(sc_done, 1)
            dve.wait_ge(sc_ps, 2)
            v.tensor_tensor(sc_s[0:TS], ps[3][0:TS, 0:P].rearrange("p (h t) -> p h t", h=H),
                            mask_s[0:TS].unsqueeze(1).to_broadcast([TS, H, TS]), ALU.mult).then_inc(sc_done, 1)
            evac(19)
            for c in range(NCH):
                if c == 2:
                    evac(20)
                for h in range(H):
                    upd = ps[UPD_BANK[h]][:, c * P:(c + 1) * P]
                    if c == 0:
                        dve.wait_ge(upd_ps, h + 1)
                        v.tensor_copy(chain[:, h, 0, :], upd).then_inc(chain_done, 1)
                    else:
                        dve.wait_ge(chain_done, H * (c - 1) + h + 1)
                        v.scalar_tensor_tensor(chain[:, h, c, :], chain[:, h, c - 1, :], dec_p[:, h, c:c + 1], upd,
                                               ALU.mult, ALU.add).then_inc(chain_done, 1)
            evac(21)
            dve.wait_ge(row_in, 16)
            for tt in range(TT):
                q, R = vn[0:ROWS[tt], tt, :], ROWS[tt]
                link(v.tensor_tensor(q, q, row[0:R, R_LNG:R_LNG + 512], ALU.mult))
                v.tensor_tensor(q, q, row[0:R, R_LNB:R_LNB + 512], ALU.add).then_inc(vn_done, 1)
            evac(22)

            def by_sequence(h):
                v.tensor_tensor(vx[h % 2], vtok[:, 2, h * P:(h + 1) * P].unsqueeze(1).to_broadcast([P, DECB, P]),
                                mask_q.unsqueeze(2).to_broadcast([P, DECB, P]), ALU.mult).then_inc(vx_done, 1)
            for h in range(2):
                by_sequence(h)
            evac(23)
            dve.wait_ge(evac_a, 3 * H)
            for h in range(H):
                dve.wait_ge(on_std, h + 1)
                link(v.reciprocal(bsum[:, h, :], bsum[:, h, :]))
                link(v.scalar_tensor_tensor(oT[:, h, :], o_raw[:, h, :], vec[:, C_HN + h:C_HN + h + 1], bsum[:, h, :],
                                            ALU.mult, ALU.mult))
                v.tensor_tensor(oT[:, h, :], oT[:, h, :], pg[:, h, :], ALU.mult).then_inc(oa_done, 1)
            dve.wait_ge(s_scaled, H)
            for h in range(H):
                for half in range(2):
                    dve.wait_ge(su_ps, 2 * h + half + 1)
                    q = st[:, 4 * half:4 * half + 4, h, :]
                    v.tensor_tensor(q, q, ps[STATE_BANK[h % 2][half]][:, :].rearrange("p (b c) -> p b c", b=4),
                                    ALU.add).then_inc(s_done, 1)
                if h < 2:
                    by_sequence(h + 2)
            def upper(dst, src):
                return v.tensor_copy(dst, src)

            def upper_unit(i):
                u = SPLIT_UNITS[i]
                dve.wait_ge(ring_in[unit_slot(u)], 16 * unit_fill(u))
                upper(w_upper[i % 3], slot[unit_slot(u)]).then_inc(w_upper_done, 1)
            dve.wait_ge(on_std, H)
            dve.wait_ge(h_done, 2 * KT)
            v.tensor_copy(memT_upper, memT).then_inc(mem_split, 1)
            for i in range(2):
                upper_unit(i)
            dve.wait_ge(evac_a, 4 * H)
            bias = row[:, R_BS:R_BS + H * T].rearrange("p (g t) -> p g t", g=H)
            for tt in range(TT):
                c0, n = tt * P, ROWS[tt]
                dst = oT[:, H:2 * H, c0:c0 + n]
                dve.wait_ge(gm_ps, tt + 1)
                link(v.tensor_tensor(dst, ps[GM_BANK[tt]][:, 0:H * n].rearrange("p (g t) -> p g t", g=H),
                                     bias[:, :, c0:c0 + n], ALU.add))
                v.tensor_tensor(dst, dst, pu[:, :, c0:c0 + n], ALU.mult).then_inc(gm_done, 1)

            dve.wait_ge(mem_split, 1)
            dve.wait_ge(proj, 32)
            v.tensor_tensor(memT_lower, memT, memT_upper, ALU.subtract).then_inc(mem_split, 1)
            dve.wait_ge(gm_done, TT)
            upper_unit(2)
            dve.wait_ge(proj, 34)
            upper_unit(3)
            link(upper(oT_upper, oT))
            v.tensor_tensor(oT_lower, oT, oT_upper, ALU.subtract).then_inc(o_split, 1)
            for i in (4, 5, 6):
                dve.wait_ge(proj, 32 + 2 * (i - 2))
                upper_unit(i)

            def residual(c, first, done):
                dve.wait_ge(proj, first + c + 1)
                v.tensor_tensor(xT[:, c, :], xT[:, c, :], ps[(first + c) % 3][:, 0:T], ALU.add).then_inc(x_add, 1)
                dve.wait_ge(x_add, done + c + 1)

            dve.wait_ge(ss_out, 16)
            for c in range(KT):
                residual(c, 40, 0)
                link(v.tensor_scalar(hX[:, c, :], xT[:, c, :], vec[:, C_X + c:C_X + c + 1], None, ALU.mult))
                link(upper(hX_upper[:, c, :], hX[:, c, :]))
                v.tensor_tensor(hX_lower[:, c, :], hX[:, c, :], hX_upper[:, c, :], ALU.subtract).then_inc(h_done, 1)
                if c % 2:
                    upper_unit(7 + c // 2)
            dve.wait_ge(std_done, 3)
            link(v.reciprocal(rstd, std))
            for c in range(KT):
                dve.wait_ge(proj, 48 + c + 1)
                v.tensor_tensor(qT[:, c, :], ps[c % 3][:, 0:T], rstd, ALU.mult).then_inc(q_ev, 1)
                if c == 1:
                    upper_unit(11)
            dve.wait_ge(q_ev, KT)
            dve.wait_ge(qm_zero, 1)
            for c in range(KT):
                v.tensor_copy(diagonal(qm, 256 * c, 0, 1),
                              qT[:, c, SEQ:T].rearrange("p (b t) -> p b t", b=DECB)).then_inc(qm_done, 1)
            for i in (12, 13, 14):
                upper_unit(i)
            for n in range(4):
                dve.wait_ge(p_score, n + 1)
                link(v.tensor_reduce(mx[:, 2 * n:2 * n + 2], ps[3 + n][:, :].rearrange("p (h m) -> p h m", h=2), AX, ALU.max))
                v.tensor_scalar(nmx[:, 2 * n:2 * n + 2], mx[:, 2 * n:2 * n + 2], -X_SCALE, None, ALU.mult).then_inc(p_max, 1)
            dve.wait_ge(p_exp, 8)
            link(v.reciprocal(prn, psm))
            for n in range(8):
                v.tensor_scalar(pr[:, n, :], pr[:, n, :], prn[:, n:n + 1], None, ALU.mult).then_inc(p_done, 1)
            dve.wait_ge(kv_used, DECB)
            link(v.tensor_reduce(smx, ps[7][:, 0:MEM], AX, ALU.max))
            v.tensor_scalar(snm, smx, -X_SCALE, None, ALU.mult).then_inc(s_max, 1)
            for k in range(2):
                dve.wait_ge(pt_ps, 3 + k)
                v.tensor_copy(prT[:, 1, 2 * k:2 * k + 2, :],
                              ps[5 + k][:, :].rearrange("p (h t) -> p h t", h=2)).then_inc(pt_done_v, 1)
            dve.wait_ge(s_exp, 1)
            link(v.reciprocal(srn, ssm))
            v.tensor_scalar(pr_s, pr_s, srn, None, ALU.mult).then_inc(sp_done, 1)
            for c in range(1, KT, 2):
                dve.wait_ge(pv_ps, c + 1)
                v.tensor_copy(oT[:, c, 0:SEQ], ps[c % 3][:, 0:SEQ]).then_inc(pv_done_v, 1)
            dve.wait_ge(st_ps, 1)
            dve.wait_ge(pm_zero, 1)
            for mt in range(2):
                for h in range(H):
                    v.tensor_copy(diagonal(pmT, 256 * (H * mt + h), 0, 1),
                                  ps[3][:, mt * P + h * TS:mt * P + (h + 1) * TS].rearrange("p (b t) -> p b t", b=DECB)
                                  ).then_inc(pm_done, 1)
            dve.wait_ge(pv_done_a, KT // 2)
            dve.wait_ge(pv_done_v, KT // 2)
            q = slice(0, SEQ)
            link(upper(oT_upper[:, :, q], oT[:, :, q]))
            v.tensor_tensor(oT_lower[:, :, q], oT[:, :, q], oT_upper[:, :, q], ALU.subtract).then_inc(o_split, 1)
            dve.wait_ge(oxT_ps, 1)
            for dc in range(2):
                v.tensor_copy(oT.rearrange("p (h c) t -> p h c t", h=H)[:, :, dc, SEQ:T],
                              ps[5][:, dc * P:(dc + 1) * P].rearrange("p (h t) -> p h t", h=H)).then_inc(oxT_done, 1)

            dve.wait_ge(oxT_done, 2)
            q = slice(SEQ, T)
            link(upper(oT_upper[:, :, q], oT[:, :, q]))
            v.tensor_tensor(oT_lower[:, :, q], oT[:, :, q], oT_upper[:, :, q], ALU.subtract).then_inc(o_split, 1)

            def split_bias(n):
                k = 1 + n // 2
                q = slice(32 * k, 32 * k + 32)
                if n == 0:
                    dve.wait_ge(b1_in, 48)
                    dve.wait_ge(pv_ps, KT)
                    link(v.tensor_copy(b1s[0:96], b1f[0:96]))
                if n < 4 and n % 2 == 0:
                    link(v.tensor_tensor(b1f[q], b1f[q], b1s[q], ALU.subtract))
                elif n < 4:
                    link(v.tensor_copy(b1s[q], b1f[q]))
                elif n == 4:
                    link(v.tensor_tensor(b1f[64:96], b1f[64:96], b1s[64:96], ALU.subtract))
                else:
                    v.tensor_copy(b1s[64:96], b1f[64:96]).then_inc(b1_split, 1)
                    dve.wait_ge(b1_split, 1)
                    v.memset(selGT, 0.0).then_inc(selgt_zero, 1)

            def x_rows(half):
                for tt in range(TT):
                    dve.wait_ge(y_ps, TT * half + tt + 1)
                    v.tensor_copy(y[0:ROWS[tt], tt, 512 * half:512 * half + 512],
                                  ps[Y_BANK[TT * half + tt]][0:ROWS[tt], :]).then_inc(y_ev, 1)
            for c in range(KT):
                residual(c, 56, KT)
                if c == 1:
                    upper_unit(15)
                if c < 6:
                    split_bias(c)
                if c == 6:
                    x_rows(0)

            dve.wait_ge(lg_ps, 1)
            v.tensor_copy(std[0:NE], ps[6][0:NE, 0:T]).then_inc(lg_done, 1)
            x_rows(1)
            dve.wait_ge(y_sq, 2 * TT)
            v.tensor_tensor(ysum, ysq[:, 0, :], ysq[:, 1, :], ALU.add).then_inc(y_sum, 1)
            v.memset(outp, 0.0).then_inc(outp_done, 2)
            dve.wait_ge(y_std, 1)
            link(v.reciprocal(yrs, yrs))
            dve.wait_ge(lt_ps, 1)
            for tt in range(TT):
                R = ROWS[tt]
                last = v.scalar_tensor_tensor(logit[0:R, tt, :], ps[5][0:R, tt * NE:(tt + 1) * NE], yrs[0:R, tt:tt + 1],
                                              br[0:R], ALU.mult, ALU.add)
            last.then_inc(logit_done, 1)
            dve.wait_ge(frow_in, 16)
            dve.wait_ge(b1_split, 1)
            dve.wait_ge(y_ev, 2 * TT)

            def token_rows(tt):
                R = ROWS[tt]
                v.scalar_tensor_tensor(htmp[tt][0:R], y[0:R, tt, :], yrs[0:R, tt:tt + 1], frow[0:R],
                                       ALU.mult, ALU.mult).then_inc(h_tok, 1)
            for tt in range(TT):
                token_rows(tt)
            dve.wait_ge(logit_done, 1)
            for tt in range(TT):
                last = v.max(top[:, tt, :], logit[:, tt, :])
            link(last)
            for tt in range(TT):
                last = v.max_index(topi[:, tt, :].bitcast(U32), top[:, tt, :], logit[:, tt, :])
            link(last)
            link(v.tensor_copy(topf, topi.bitcast(U32)))
            v.tensor_tensor(gate, top[:, :, 0:TOPK], top[:, :, 0:1].to_broadcast([P, TT, TOPK]),
                            ALU.subtract).then_inc(gate_in, 1)
            for tt in range(TT):
                last = v.tensor_tensor(pick_t[:, tt], iota_e.unsqueeze(1).to_broadcast([P, TOPK, NE]),
                                       topf[:, tt, 0:TOPK].unsqueeze(2).to_broadcast([P, TOPK, NE]), ALU.is_equal)
            link(last)
            link(v.tensor_reduce(gates, pick_t.rearrange("p t k e -> p t e k"), AX, ALU.add))
            v.tensor_tensor(chosen, gates, valid, ALU.mult).then_inc(chosen_done, 1)

            def third_part(tt):
                R = ROWS[tt]
                dve.wait_ge(h_mid, tt + 1)
                v.tensor_tensor(hx[0:R, 2, tt, :], htmp[tt][0:R], hx[0:R, 1, tt, :], ALU.subtract).then_inc(h_split, 1)
            dve.wait_ge(pos_ps, 1)
            pos = ps[6][:, 0:TT * NE].rearrange("p (t e) -> p t e", t=TT)
            link(v.scalar_tensor_tensor(place[:, :, 0:NE], pos, 1.0, chosen, ALU.add, ALU.mult))
            link(v.tensor_reduce(most, ps[6][:, TT * NE:(TT + 1) * NE], AX, ALU.max))
            v.tensor_copy(most_i, most).then_inc(most_done, 1)
            link(v.tensor_scalar(place[:, :, 0:NE], place[:, :, 0:NE], -1.0, None, ALU.add))
            link(v.tensor_scalar(place[:, :, NE:NE + 2], place[:, :, 0:2], -float(CAP), None, ALU.add))

            def select_pair(e):
                for tt in range(TT):
                    for half in range(2):
                        last = v.tensor_scalar(sel[:, tt, CAP * half:CAP * half + CAP], iota_slot[:, 0:CAP],
                                               place[:, tt, bass.ds(e + half, 1)], None, ALU.is_equal)
                last.then_inc(sel_done, 1)

            def pick_bias(e, parity):
                v.tensor_scalar(oh[parity][0:96], ones[0:96, 0:CAP], pick_e[0:96, bass.ds(e, 1)], None,
                                ALU.mult).then_inc(oh_done, 1)

            select_pair(0)
            pick_bias(0, 0)
            for tt in range(TT):
                third_part(tt)
            dve.wait_ge(gate_exp, 1)
            link(v.tensor_reduce(gsum, gate, AX, ALU.add))
            link(v.reciprocal(gsum, gsum))
            link(v.tensor_tensor(gate, gate, gsum.unsqueeze(2).to_broadcast([P, TT, TOPK]), ALU.mult))
            for tt in range(TT):
                last = v.tensor_tensor(pick_t[:, tt], pick_t[:, tt],
                                       gate[:, tt].unsqueeze(2).to_broadcast([P, TOPK, NE]), ALU.mult)
            link(last)
            link(v.tensor_reduce(gates, pick_t.rearrange("p t k e -> p t e k"), AX, ALU.add))
            v.tensor_tensor(gates, gates, valid, ALU.mult).then_inc(gates_done, 1)

            v.memset(selG, 0.0).then_inc(selgt_ps, 1)
            v.memset(most, 0.0).then_inc(comb_free, 2)

            def add_combined(c, pieces=range(2 * TT)):
                if pieces[0] == 0:
                    dve.wait_ge(comb_free, 2 * TT * c + 2)
                for q in pieces:
                    tt, half = q // 2, q % 2
                    R = ROWS[tt]
                    dst = y[0:R, tt, 512 * half:512 * half + 512]
                    dve.wait_ge(comb_ps, 2 * TT * c + q + 1)
                    v.tensor_tensor(dst, dst, ps[6 + q % 2][0:R, :], ALU.add).then_inc(comb_free, 1)

            def turn(i, g, r):
                for j in range(BODY):
                    n, e = g * BODY + j, i * BODY + j
                    pick_bias(e + 1, (j + 1) % 2)
                    dve.wait_ge(selgt_ps, n + 1)
                    for tt in range(TT):
                        last = v.tensor_scalar(selG[:, tt, :], iota_slot, place[:, tt, bass.ds(e, 1)],
                                               gates[:, tt, bass.ds(e, 1)], ALU.is_equal, ALU.mult)
                    last.then_inc(selg_done, 1)
                    if j % 2 == 0:
                        dve.wait_ge(xg_ps, g * BODY + j + 2)
                        select_pair(e + 2)
                    add_combined(n + r, range(2 * TT) if j % 2 == 0 else range(3))
                    dve.wait_ge(units_used, n * EXP_UNITS + W1_UNITS)
                    v.tensor_scalar(glu, ps[0][:, :], LIMIT, None, ALU.min).then_inc(glu_done, 1)
                    v.tensor_scalar(lin, ps[1][:, :], LIMIT, -LIMIT, ALU.min, ALU.max).then_inc(lin_done, 1)
                    dve.wait_ge(glu_done, n + 1)
                    dve.wait_ge(lin_done, n + 1)
                    v.scalar_tensor_tensor(lin, lin, 1.0, glu, ALU.add, ALU.mult).then_inc(prod_done, 1)
                    dve.wait_ge(prod_done, n + 1)
                    dve.wait_ge(sig_done, n + 1)
                    v.tensor_tensor(act, lin, sig, ALU.mult).then_inc(act_done, 1)
                    if j % 2:
                        add_combined(n + r, range(3, 2 * TT))

            def last_combine(g, r):
                add_combined(g * BODY + r)
                dve.wait_ge(comb_free, 2 * TT * (g * BODY + r + 1) + 2)

            def next_places():
                v.tensor_scalar(place, place, -float(CAP), None, ALU.add).then_inc(round_step, 1)

            with dve.Fori(0, TURNS) as i:
                turn(i, i, 0)
            last_combine(TURNS, 0)
            next_places()
            fullest = dve.value_load(most_i[0:1, 0:1], min_val=0, max_val=T)

            def one_round(r):
                dve.wait_ge(selgt_ps, r * NE + 1)
                dve.wait_ge(round_step, r)
                v.memset(selGT, 0.0).then_inc(selgt_done, 1)
                with dve.Fori(0, TURNS) as i:
                    turn(i, r * TURNS + i, r)
                last_combine((r + 1) * TURNS, r)
                next_places()
            further_rounds(dve, fullest, one_round)
            v.memset(most, 0.0).then_inc(rounds_done, 1)
            dve.wait_ge(grow_in, 16)
            for tt in range(TT):
                R = ROWS[tt]
                dve.wait_ge(fin_std, tt + 1)
                link(v.reciprocal(yrs[0:R, tt:tt + 1], yrs[0:R, tt:tt + 1]))
                v.scalar_tensor_tensor(y[0:R, tt, :], y[0:R, tt, :], yrs[0:R, tt:tt + 1], frow[0:R],
                                       ALU.mult, ALU.mult).then_inc(y_ready, 1)

        @block.tensor
        def _(pe):
            t = nc.tensor

            def sums(i, n):
                pe.wait_ge(sq_sum, i + 1 if i < 2 else 2 + KT - 1)
                t.matmul(ps[7][:, 0:n], ones, sq[i][:, 0, :], start=True, stop=True).then_inc(ss_done, 1)

            def unit_ready(u):
                pe.wait_ge(ring_in[unit_slot(u)], 16 * unit_fill(u))
                return slot[unit_slot(u)]

            def project(u, c, moving, n, first_h):
                w = unit_ready(u).rearrange("p (k c) -> p k c", k=KT)
                for k in range(KT):
                    if c == 0:
                        pe.wait_ge(h_done, first_h + k + 1)
                    last = t.matmul(ps[c % 3][:, 0:n], w[:, k, (c % 2) * P:(c % 2 + 1) * P], moving[:, k, :],
                                    start=(k == 0), stop=(k == KT - 1))
                last.then_inc(proj, 1)

            def token_major(src, evacuated):
                if evacuated:
                    pe.wait_ge(tok_done, evacuated)
                for tt in range(TT):
                    R = ROWS[tt]
                    for h in range(H):
                        last = t.transpose(ps[4 + tt][0:R, h * P:(h + 1) * P], src[:, h, tt * P:tt * P + R], ident)
                    last.then_inc(tok_ps, 1)

            def freed(c):
                if c < 0:
                    return
                for first, done, n in ((56, x_add, KT), (48, q_ev, 0), (40, x_add, 0), (24, evac_a, 16), (0, evac_v, 0)):
                    if c >= first:
                        pe.wait_ge(done, n + c - first + 1)
                        return

            def w_in_chunks(*chunks):
                for c in chunks:
                    freed(c - 3)
                    project(U_IN + c // 2, c, hT, T, 0)

            w_in_chunks(0)
            pe.wait_ge(consts, 1)
            sums(0, T)
            w_in_chunks(1, 2, 3, 4, 5, 6, 7, 8)
            pe.wait_ge(evac_v, 8)
            token_major(pi, 0)
            pe.wait_ge(std_done, 1)
            sums(1, MEM)
            w_in_chunks(9, 10, 11, 12)
            pe.wait_ge(evac_v, 12)
            token_major(pv, TT)
            w_in_chunks(13, 14, 15, 16)
            pe.wait_ge(k2_done, 1)
            token_major(k2, 2 * TT)
            w_in_chunks(17, 18)
            pe.wait_ge(std_done, 2)
            pe.wait_ge(qk1_done, 2)
            for tt in range(2):
                for h in range(H):
                    for half in range(2):
                        q = slice(tt * P + CH * half, tt * P + CH * half + CH)
                        last = t.matmul(ps[7][CH * half:CH * half + CH, (H * tt + h) * CH:(H * tt + h + 1) * CH],
                                        k1[:, h, q], q1[:, h, q], start=True, stop=True)
            last.then_inc(sc_ps, 1)
            for h in range(H):
                last = t.matmul(ps[3][0:TS, h * TS:(h + 1) * TS], k1[:, h, SEQ:T], q1[:, h, SEQ:T], start=True, stop=True)
            last.then_inc(sc_ps, 1)
            w_in_chunks(19)
            pe.wait_ge(tok_done, 3 * TT)
            pe.wait_ge(vsplit_done, 4)
            pe.wait_ge(sc_done, 3)
            for h in range(H):
                for tt in range(2):
                    last = t.matmul(ps[UPD_BANK[h]][:, tt * 256:(tt + 1) * 256], ktok[:, tt, h * P:(h + 1) * P],
                                    vsplit[:, H * tt + h, :], start=True, stop=True)
                last.then_inc(upd_ps, 1)
            w_in_chunks(20, 21)
            pe.wait_ge(q2_done, 1 + H)
            pe.wait_ge(chain_done, H * NCH)
            for h in range(H):
                bank, at = ps[7 if h < 2 else 4], (h % 2) * SEQ
                for tt in range(2):
                    t.matmul(bank[:, at + tt * P:at + (tt + 1) * P], vtok[:, tt, h * P:(h + 1) * P],
                             sc_p[:, H * tt + h, :], start=True, stop=False)
                    for c in range(max(1, 2 * tt), 2 * tt + 2):
                        last = t.matmul(bank[:, at + c * CH:at + (c + 1) * CH], chain[:, h, c - 1, :],
                                        q2[:, h, c * CH:(c + 1) * CH], start=False, stop=(c == 2 * tt + 1))
                if h % 2:
                    last.then_inc(o_ps, 1)
            pe.wait_ge(consts, 3)
            pe.wait_ge(st_in, 16)
            for h in range(H):
                out = ps[5][TS * h:TS * (h + 1), 0:P]
                t.matmul(out, sc_s[:, h, :], vtok[:, 2, h * P:(h + 1) * P], start=True, stop=False)
                for b in range(DECB):
                    last = t.matmul(out, q2m[:, h, b * TS:(b + 1) * TS], st[:, b, h, :], start=False, stop=(b == DECB - 1))
            last.then_inc(os_ps, 1)
            w_in_chunks(22)
            pe.wait_ge(os_done, 1)
            t.transpose(ps[6][:, 0:P], o_s, ident).then_inc(os_ps, 1)
            w_in_chunks(23)
            pe.wait_ge(osq_done, 1)
            for h in range(H):
                t.matmul(ps[NORM_BANK[h]][:, 0:T], ones, k2[:, h, :], start=True, stop=True).then_inc(on_ps, 1)

            def key_chunks(*chunks):
                for c in chunks:
                    freed(24 + c - 3)
                    project(U_XK + c // 2, c, memT, MEM, KT)

            def state_updates(h):
                pe.wait_ge(vx_done, h + 1)
                if h < 2:
                    pe.wait_ge(on_std, 3 if h else 1)
                else:
                    pe.wait_ge(s_done, 2 * (h - 1))
                for half in range(2):
                    t.matmul(ps[STATE_BANK[h % 2][half]][:, :], ktok[:, 2, h * P:(h + 1) * P],
                             vx[h % 2][:, 4 * half:4 * half + 4, :].rearrange("p b c -> p (b c)"),
                             start=True, stop=True).then_inc(su_ps, 1)

            key_chunks(0)
            state_updates(0)
            state_updates(1)
            key_chunks(1, 2, 3, 4)
            state_updates(2)
            state_updates(3)
            key_chunks(5)
            pe.wait_ge(on_std, H)
            pe.wait_ge(s_done, 6)
            for tt in range(TT):
                n = ROWS[tt]
                pe.wait_ge(vn_done, tt + 1)
                for g in range(H):
                    last = t.matmul(ps[GM_BANK[tt]][:, g * n:(g + 1) * n], vn[:, tt, g * P:(g + 1) * P],
                                    gw[:, g, :] if tt < 2 else gwc[:, g, :], start=True, stop=True)
                last.then_inc(gm_ps, 1)
            key_chunks(6, 7)
            def split_unit(i):
                pe.wait_ge(w_split, i + 1)
                return (x.rearrange("p (k c) -> p k c", k=KT)
                        for x in (w_upper[i % 3], slot_r[unit_slot(SPLIT_UNITS[i])]))

            pe.wait_ge(mem_split, 1)
            for c in range(8):
                w_hi, w_lo = split_unit(c // 2)
                col = slice((c % 2) * P, (c % 2 + 1) * P)
                freed(32 + c - 3)
                for n, (x, w) in enumerate(((memT_upper, w_lo), (memT_upper, w_hi), (memT_lower, w_hi))):
                    if c == 0 and n == 2:
                        pe.wait_ge(mem_split, 2)
                    for k in range(KT):
                        last = t.matmul(ps[(32 + c) % 3][:, 0:256], x[:, k, col], w[:, k, :],
                                        start=(k == 0 and n == 0), stop=(k == KT - 1 and n == 2))
                last.then_inc(proj, 1)
            def project_split(i, c, hi, lo, bank, h_first=None):
                w_hi, w_lo = split_unit(i)
                col = slice((c % 2) * P, (c % 2 + 1) * P)
                for k in range(KT):
                    if h_first is not None and c == 0:
                        pe.wait_ge(h_done, h_first + k + 1)
                    for n, (w, x) in enumerate(((w_lo, hi), (w_hi, lo), (w_hi, hi))):
                        last = t.matmul(ps[bank][:, 0:T], w[:, k, col], x[:, k, :], start=(k == 0 and n == 0),
                                        stop=(k == KT - 1 and n == 2))
                last.then_inc(proj, 1)

            pe.wait_ge(oa_done, H)
            pe.wait_ge(gm_done, TT)
            pe.wait_ge(o_split, 1)
            for c in range(KT):
                freed(40 + c - 3)
                project_split(4 + c // 2, c, oT_upper, oT_lower, (40 + c) % 3)
                if c == 3:
                    pe.wait_ge(evac_a, 16 + KT)
                    pe.wait_ge(s_done, 2 * H)
                    for n in range(4):
                        mt, b = n // 2, n % 2
                        for a in range(4):
                            last = t.transpose(ps[3 + n][:, a * P:(a + 1) * P], kT[:, 4 * b + a, mt * P:(mt + 1) * P], ident)
                        last.then_inc(km_ps, 1)
            for c in range(KT):
                freed(48 + c - 3)
                project_split(8 + c // 2, c, hX_upper, hX_lower, c % 3, 2 * KT)
                if c == 0:
                    sums(2, T)
            pe.wait_ge(q_ev, KT)
            pe.wait_ge(km_done, 4)
            for n in range(4):
                tt, hp = n // 2, n % 2
                for a in range(2):
                    for dc in range(2):
                        c = 2 * (2 * hp + a) + dc
                        last = t.matmul(ps[3 + n][:, a * MEM:(a + 1) * MEM], qT[:, c, tt * P:(tt + 1) * P], kT[:, c, :],
                                        start=(dc == 0), stop=(dc == 1))
                last.then_inc(p_score, 1)
            pe.wait_ge(std_done, 3)
            pe.wait_ge(qm_done, KT)
            for b in range(DECB):
                w = unit_ready(U_KC + b).rearrange("p (k m) -> p k m", k=KT)
                for dc in range(2):
                    for h in range(H):
                        c = 2 * h + dc
                        last = t.matmul(ps[7][TS * h:TS * (h + 1), 0:MEM], qm[:, c, b * TS:(b + 1) * TS], w[:, c, :],
                                        start=(b == 0 and dc == 0), stop=(b == DECB - 1 and dc == 1))
                last.then_inc(kv_used, 1)
            pe.wait_ge(p_done, 8)
            for k in range(4):
                mt, hp = k // 2, k % 2
                for a in range(2):
                    for tt in range(2):
                        last = t.transpose(ps[3 + k][:, a * SEQ + tt * P:a * SEQ + (tt + 1) * P],
                                           pr[:, H * tt + 2 * hp + a, mt * P:(mt + 1) * P], ident)
                last.then_inc(pt_ps, 1)
            pe.wait_ge(pt_done_a, 2)
            pe.wait_ge(pt_done_v, 2)
            pe.wait_ge(sp_done, 1)
            for mt in range(2):
                last = t.transpose(ps[3][:, mt * P:(mt + 1) * P], pr_s[:, mt * P:(mt + 1) * P], ident)
            last.then_inc(st_ps, 1)
            for c in range(KT):
                if c >= 3:
                    pe.wait_ge(pv_done_v if (c - 3) % 2 else pv_done_a, (c - 3) // 2 + 1)
                for mt in range(2):
                    last = t.matmul(ps[c % 3][:, 0:SEQ], vM[:, mt, c * P:(c + 1) * P], prT[:, mt, c // 2, :],
                                    start=(mt == 0), stop=(mt == 1))
                last.then_inc(pv_ps, 1)
            pe.wait_ge(pm_done, 8)
            for b in range(DECB):
                w = unit_ready(U_VC + b).rearrange("p (m c) -> p m c", m=2)
                for mt in range(2):
                    for h in range(H):
                        last = t.matmul(ps[4][TS * h:TS * (h + 1), 0:256], pmT[:, mt, h, b * TS:(b + 1) * TS],
                                        w[:, mt, h * 256:(h + 1) * 256],
                                        start=(b == 0 and mt == 0), stop=(b == DECB - 1 and mt == 1))
                last.then_inc(kv_used, 1)
            pe.wait_ge(ox_done, 1)
            for dc in range(2):
                last = t.transpose(ps[5][:, dc * P:(dc + 1) * P], o_x[:, dc * P:(dc + 1) * P], ident)
            last.then_inc(oxT_ps, 1)
            pe.wait_ge(pv_done_a, KT // 2)
            pe.wait_ge(pv_done_v, KT // 2)
            pe.wait_ge(oxT_done, 2)
            pe.wait_ge(o_split, 3)
            pe.wait_ge(consts, 3)

            def router(k):
                pe.wait_ge(x_add, KT + k + 1)
                return t.matmul(ps[6][0:NE, 0:T], wr[:, k, :], xT[:, k, :], start=(k == 0), stop=(k == KT - 1))

            def x_rows(half):
                for tt in range(TT):
                    R, n = ROWS[tt], TT * half + tt
                    if n > TT:
                        pe.wait_ge(y_ev, n - TT)
                    for k in range(4):
                        last = t.transpose(ps[Y_BANK[n]][0:R, k * P:(k + 1) * P],
                                           xT[:, 4 * half + k, tt * P:tt * P + R], ident)
                    last.then_inc(y_ps, 1)

            for c in range(KT):
                if c >= 3:
                    freed(56 + c - 3)
                project_split(12 + c // 2, c, oT_upper, oT_lower, (56 + c) % 3)
                if c >= 2:
                    router(c - 2)
                if c == 5:
                    x_rows(0)
            router(KT - 2)
            router(KT - 1).then_inc(lg_ps, 1)
            x_rows(1)
            pe.wait_ge(lg_done, 1)
            pe.wait_ge(y_ev, TT)
            for tt in range(TT):
                R = ROWS[tt]
                last = t.transpose(ps[5][0:R, tt * NE:(tt + 1) * NE], std[0:NE, tt * P:tt * P + R], ident[0:NE, 0:NE])
            last.then_inc(lt_ps, 1)
            pe.wait_ge(chosen_done, 1)
            for tt in range(TT):
                for s in range(tt + 1):
                    t.matmul(ps[6][:, tt * NE:(tt + 1) * NE], tri if s == tt else ones_b, chosen[:, s, :],
                             start=(s == 0), stop=(s == tt))
            for s in range(TT):
                last = t.matmul(ps[6][:, TT * NE:(TT + 1) * NE], ones_b, chosen[:, s, :], start=(s == 0), stop=(s == TT - 1))
            last.then_inc(pos_ps, 1)

            def gather():
                for d in range(KT):
                    for tt in range(TT):
                        for s in range(3):
                            last = t.matmul(ps[4 + d // 4][:, (d % 4) * P:(d % 4 + 1) * P],
                                            hx[:, s, tt, d * P:(d + 1) * P], sel[:, tt, :],
                                            start=(tt == 0 and s == 0), stop=(tt == TT - 1 and s == 2))
                    if d % 4 == 3:
                        last.then_inc(xg_ps, 1)

            pe.wait_ge(sel_done, 1)
            pe.wait_ge(h_split, 3)
            pe.wait_ge(y_ev, 2 * TT)
            gather()
            pe.wait_ge(gates_done, 1)
            for tt in range(TT):
                last = t.transpose(ps[7][0:NE, tt * P:(tt + 1) * P], gates[:, tt, :], ident)
            last.then_inc(gt_ps, 1)
            def combine(c, pieces=range(2 * TT)):
                for q in pieces:
                    tt, half = q // 2, q % 2
                    pe.wait_ge(comb_free, 2 * TT * c + q + 1)
                    t.matmul(ps[6 + half][0:ROWS[tt], :], selGT[:, tt * P:tt * P + ROWS[tt]],
                             outp[:, half * 512:(half + 1) * 512], start=True, stop=True).then_inc(comb_ps, 1)

            def turn(g, r):
                for j in range(BODY):
                    n = g * BODY + j
                    slots = xg[(j // 2) % 2][:, :, CAP * (j % 2):CAP * (j % 2) + CAP]

                    def expert_unit(u):
                        s, fill = (EXP_UNITS * j + u + PRE) % SLOTS, (EXP_UNITS * j + u) // SLOTS
                        pe.wait_ge(ring_in[s], (BODY * EXP_UNITS // SLOTS * g + (fills(s) + fill + 1)) * 16)
                        return slot[s]

                    pe.wait_ge(oh_done, n + 1)
                    parts = [(ps[q // 2][CAP * (q % 2):CAP * (q % 2) + CAP, :], slice(512 * q, 512 * q + 512)) for q in range(4)]
                    for out, col in parts:
                        t.matmul(out, oh[j % 2][0:96], b1s[0:96, col], start=True, stop=False)
                    for k in range(KT):
                        w = expert_unit(k)
                        if k % 4 == 0:
                            pe.wait_ge(xg_done, g * BODY + 2 * (j // 2) + k // 4 + 1)
                        for out, col in parts:
                            last = t.matmul(out, slots[:, k, :], w[:, col], start=False, stop=(k == KT - 1))
                        last.then_inc(units_used, 1)
                        if k == 3:
                            pe.wait_ge(outp_done, 2 * (n + 1))
                            pe.wait_ge(selgt_done, n + r + 1)
                            combine(n + r, range(2 * TT) if j % 2 == 0 else range(3))
                    if j % 2:
                        combine(n + r, range(3, 2 * TT))
                    if j % 2 == 0:
                        pe.wait_ge(sel_done, g * (BODY // 2) + j // 2 + 2)
                        gather()
                    pe.wait_ge(act_done, n + 1)
                    if j % 2 == 0:
                        pe.wait_ge(xg_done, g * BODY + 2 * (j // 2 + 2))
                    for a in range(4):
                        last = t.transpose(ps[4][:, a * P:(a + 1) * P], act[:, a * P:(a + 1) * P], ident)
                    last.then_inc(actt_ps, 1)
                    pe.wait_ge(selg_done, n + 1)
                    for tt in range(TT):
                        last = t.transpose(ps[5][:, tt * P:(tt + 1) * P], selG[:, tt, :], ident)
                    last.then_inc(selgt_ps, 1)
                    pe.wait_ge(actt_done, n + 1)
                    for a in range(W2_UNITS):
                        w = expert_unit(W1_UNITS + a).rearrange("p (h c) -> p h c", h=2)
                        for ds in range(2):
                            for cg in range(2):
                                last = t.matmul(ps[2 + ds][CAP * cg:CAP * cg + CAP, :],
                                                actT[:, a * P + CAP * cg:a * P + CAP * cg + CAP],
                                                w[:, cg, 512 * ds:512 * ds + 512], start=(a == 0), stop=(a == W2_UNITS - 1))
                        last.then_inc(units_used, 1)

            def last_combine(g, r):
                pe.wait_ge(outp_done, 2 * (g * BODY + 1))
                pe.wait_ge(selgt_done, g * BODY + r + 1)
                combine(g * BODY + r)

            pe.wait_ge(b1_split, 1)
            pe.wait_ge(b2_in, 16)
            with pe.Fori(0, TURNS) as i:
                turn(i, 0)
            last_combine(TURNS, 0)
            pe.wait_ge(most_done, 1)
            fullest = pe.value_load(most_i[0:1, 0:1], min_val=0, max_val=T)

            def one_round(r):
                with pe.Fori(0, TURNS) as i:
                    turn(r * TURNS + i, r)
                last_combine((r + 1) * TURNS, r)
            further_rounds(pe, fullest, one_round)


def kernel(x_prompt, x_sample, mem_prompt, state_hgrn, cache_mem_k, cache_mem_v, norm_mix_g, w_in,
           hgrn_lb_logits, hgrn_norm_g, gmlp_ln_g, gmlp_ln_b, gmlp_w_s, gmlp_b_s, w_out, norm_x_g,
           norm_mem_g, w_xq, w_xk, w_xv, w_xo, norm_ffn_g, w_router, b_router, w1, b1, w2, b2, norm_final_g):
    import numpy as np
    import concourse.bacc as bacc
    from concourse.bass_utils import run_bass_kernel_spmd

    def per_partition(vector):
        return np.asarray(vector).reshape(-1, P).T

    xp, xs, mem = np.asarray(x_prompt)[0], np.asarray(x_sample).reshape(TS, D), np.asarray(mem_prompt)[0]
    cols = np.concatenate([per_partition(norm_mix_g), per_partition(norm_mem_g), per_partition(norm_x_g),
                           per_partition(norm_ffn_g), per_partition(hgrn_lb_logits), per_partition(hgrn_norm_g)], axis=1)
    b_s, w_s = np.asarray(gmlp_b_s)[0], np.asarray(gmlp_w_s)[0]
    bias = np.concatenate([np.tile(b_s, (1, SEQ // P)), np.tile(b_s[:, :DECL], (1, DECB))], axis=1)
    rows = np.concatenate([np.asarray(gmlp_ln_g).reshape(-1), np.asarray(gmlp_ln_b).reshape(-1), bias.reshape(-1)])
    w_st = w_s.transpose(2, 0, 1)
    k_t = np.asarray(cache_mem_k)[0].reshape(DECB, MEM, D).transpose(0, 2, 1)
    arrays = dict(
        x_t=np.concatenate([xp, xs]).T, mem_t=mem.T, cols=cols, rows=rows,
        b_router=np.asarray(b_router)[0], w_router=w_router[0], w_in=w_in[0], w_xk=w_xk[0],
        w_xv=w_xv[0], w_out=w_out[0], w_xq=w_xq[0], w_xo=w_xo[0], k_t=k_t,
        v_c=np.asarray(cache_mem_v)[0].reshape(DECB, MEM, D), s0=np.asarray(state_hgrn).reshape(DECB * H, P, P),
        gw_t=w_st, gwc_t=np.tile(w_st[:DECL, :, :DECL], (DECB, 1, DECB)), ffn_g=norm_ffn_g[0],
        fin_g=norm_final_g, w1=w1[0], b1=b1[0], w2=w2[0], b2=b2[0])
    shapes = dict(y_p=[SEQ, D], y_s=[TS, D], s_p=[H, P, P], mk_p=[MEM, D], mv_p=[MEM, D], s_s=[DECB * H, P, P],
                  gv_s=[TS, H * P])
    nc = bacc.Bacc("TRN2", target_bir_lowering=False, num_devices=1)
    arrays = {name: np.ascontiguousarray(a) for name, a in arrays.items()}
    dram = {name: nc.dram_tensor(name, a.shape, mybir.dt.from_np(a.dtype), kind="ExternalInput").ap()
            for name, a in arrays.items()}
    dram.update({name: nc.dram_tensor(name, shape, F32, kind="ExternalOutput").ap() for name, shape in shapes.items()})
    hybrid_decoder_step(nc, **dram)
    out = run_bass_kernel_spmd(nc, [arrays], core_ids=[0]).results[0]
    return (out["y_p"].reshape(1, SEQ, D), out["y_s"].reshape(DECB, DECL, D), out["s_p"].reshape(1, 1, H, P, P),
            out["mk_p"].reshape(1, 1, MEM, H, MEM), out["mv_p"].reshape(1, 1, MEM, H, MEM),
            out["s_s"].reshape(1, DECB, H, P, P), out["gv_s"].reshape(1, DECB, DECL, H, P))
```
